# Optimizing a Trainium2 kernel written in Bass

```python
import jax, jax.numpy as jnp
from jax import lax
import numpy as np

D_MODEL = 1024
BATCH = 1
SEQ = 512
DEPTH = 1

N_MIXERS = 2
ATTN_HEAD_DIM = 64
ATTN_HEADS = D_MODEL // ATTN_HEAD_DIM
DILATION_PAIRS = ((128, 1), (512, 4), (2048, 16))
ATTN_BLOCK = 128
MLSTM_HEADS = 4
MLSTM_V_DIM = D_MODEL // MLSTM_HEADS
MLSTM_QK_DIM = MLSTM_V_DIM // 2
MLSTM_CHUNK = 64
CONV_WIDTH = 4
N_GROUPS = 8
EXPERTS_PER_GROUP = 8
N_EXPERTS = N_GROUPS * EXPERTS_PER_GROUP
TOP_K_IN_GROUP = 2
EXPERT_FF = D_MODEL // 2
MOE_BLOCK = 256
NORM_EPS = 1e-6

kernel_name = "hybrid_dilated_attn_mlstm_hmoe"

F32 = jnp.float32

def rms_norm(x, gain):
    xf = x.astype(F32)
    y = xf * lax.rsqrt(jnp.mean(xf * xf, axis=-1, keepdims=True) + NORM_EPS)
    return (y * gain.astype(F32)).astype(x.dtype)

def rms_norm_f32(x, gain):
    xf = x.astype(F32)
    return xf * lax.rsqrt(jnp.mean(xf * xf, axis=-1, keepdims=True) + NORM_EPS) * gain.astype(F32)

def dilated_branch(q, k, v, window, dilation):
    B_, S_, H_, Dh = q.shape
    n_back = window // dilation
    blk = ATTN_BLOCK
    span = dilation * blk
    S_pad = -(-S_ // span) * span
    nb = S_pad // span
    pad = ((0, 0), (0, S_pad - S_), (0, 0), (0, 0))

    def split(t):
        return jnp.pad(t, pad).reshape(B_, nb, blk, dilation, H_, Dh)

    def band(t):
        prev = jnp.concatenate([jnp.zeros_like(t[:, :1]), t[:, :-1]], axis=1)
        return jnp.concatenate([prev, t], axis=2)

    qb = split(q)
    kband = band(split(k))
    vband = band(split(v))
    s = jnp.einsum('bnqrhd,bnkrhd->bnrhqk', qb, kband) * (Dh ** -0.5)
    qi = jnp.arange(blk)[:, None]
    ki = jnp.arange(2 * blk)[None, :]
    dist = blk + qi - ki
    valid = (dist >= 0) & (dist <= n_back)
    valid = valid[None] & ((jnp.arange(nb)[:, None, None] > 0) | (ki >= blk)[None])
    s = jnp.where(valid[None, :, None, None], s, -jnp.inf)
    mx = jnp.max(s, axis=-1, keepdims=True)
    p = jnp.exp(s - mx)
    l = jnp.sum(p, axis=-1, keepdims=True)
    o = jnp.einsum('bnrhqk,bnkrhd->bnrhqd', p, vband) / l
    o = o.transpose(0, 1, 4, 2, 3, 5).reshape(B_, S_pad, H_, Dh)[:, :S_]
    lse = (mx[..., 0] + jnp.log(l[..., 0])).transpose(0, 1, 4, 2, 3).reshape(B_, S_pad, H_)[:, :S_]
    return o, lse

def dilated_attention_mixer(h, w_in, q_gain, k_gain, w_out):
    B_, S_, _ = h.shape
    qkv = (h @ w_in).reshape(B_, S_, 3, ATTN_HEADS, ATTN_HEAD_DIM).astype(F32)
    q = rms_norm_f32(qkv[:, :, 0], q_gain)
    k = rms_norm_f32(qkv[:, :, 1], k_gain)
    v = qkv[:, :, 2]
    outs, lses = [], []
    for window, dilation in DILATION_PAIRS:
        o, l = dilated_branch(q, k, v, window, dilation)
        outs.append(o)
        lses.append(l)
    wts = jax.nn.softmax(jnp.stack(lses), axis=0)
    o = jnp.einsum('gbsh,gbshd->bshd', wts, jnp.stack(outs))
    return o.reshape(B_, S_, ATTN_HEADS * ATTN_HEAD_DIM).astype(h.dtype) @ w_out

def causal_depthwise_conv(x, w):
    c = x.shape[-1]
    return lax.conv_general_dilated(
        x, w[:, None, :].astype(x.dtype), window_strides=(1,), padding=((CONV_WIDTH - 1, 0),),
        dimension_numbers=('NWC', 'WIO', 'NWC'), feature_group_count=c)

def mlstm_chunkwise(q, k, v, logi, logf):
    B_, S_, NH, DK = q.shape
    DV = v.shape[-1]
    L = MLSTM_CHUNK
    nc = S_ // L

    def chunks4(t):
        return t.reshape(B_, nc, L, NH, t.shape[-1]).transpose(1, 0, 3, 2, 4)

    def chunks3(t):
        return t.reshape(B_, nc, L, NH).transpose(1, 0, 3, 2)

    causal = jnp.tril(jnp.ones((L, L), dtype=bool))

    def step(carry, inp):
        C, n, m = carry
        qc, kc, vc, ic, fc = inp
        b = jnp.cumsum(fc, axis=-1)
        D = jnp.where(causal, b[..., :, None] - b[..., None, :] + ic[..., None, :], -jnp.inf)
        m_inter = b + m[..., None]
        m_t = jnp.maximum(m_inter, jnp.max(D, axis=-1))
        s = jnp.einsum('bhtd,bhsd->bhts', qc, kc) * jnp.exp(D - m_t[..., None])
        w_inter = jnp.exp(m_inter - m_t)
        num = jnp.einsum('bhts,bhsv->bhtv', s, vc) + w_inter[..., None] * jnp.einsum('bhtd,bhdv->bhtv', qc, C)
        den = jnp.sum(s, axis=-1) + w_inter * jnp.einsum('bhtd,bhd->bht', qc, n)
        h = num / jnp.maximum(jnp.abs(den), jnp.exp(-m_t))[..., None]
        bL = b[..., -1]
        g = bL[..., None] - b + ic
        m_new = jnp.maximum(bL + m, jnp.max(g, axis=-1))
        decay = jnp.exp(bL + m - m_new)
        wk = jnp.exp(g - m_new[..., None])[..., None] * kc
        C_new = decay[..., None, None] * C + jnp.einsum('bhsd,bhsv->bhdv', wk, vc)
        n_new = decay[..., None] * n + jnp.sum(wk, axis=-2)
        return (C_new, n_new, m_new), h

    init = (jnp.zeros((B_, NH, DK, DV), F32), jnp.zeros((B_, NH, DK), F32), jnp.zeros((B_, NH), F32))
    _, hs = lax.scan(step, init, (chunks4(q), chunks4(k), chunks4(v), chunks3(logi), chunks3(logf)))
    return hs.transpose(1, 0, 3, 2, 4).reshape(B_, S_, NH, DV)

def mlstm_mixer(h, w_in, conv_w, conv_b, gate_b, h_gain, w_out):
    B_, S_, _ = h.shape
    qk_w = MLSTM_HEADS * MLSTM_QK_DIM
    v_w = MLSTM_HEADS * MLSTM_V_DIM
    proj = h @ w_in
    qk = proj[..., :2 * qk_w]
    v = proj[..., 2 * qk_w:2 * qk_w + v_w]
    og = proj[..., 2 * qk_w + v_w:2 * qk_w + 2 * v_w]
    gates = proj[..., 2 * qk_w + 2 * v_w:].astype(F32) + gate_b.astype(F32)
    qk = jax.nn.silu(causal_depthwise_conv(qk, conv_w) + conv_b.astype(qk.dtype)).astype(F32)
    q = qk[..., :qk_w].reshape(B_, S_, MLSTM_HEADS, MLSTM_QK_DIM)
    k = qk[..., qk_w:].reshape(B_, S_, MLSTM_HEADS, MLSTM_QK_DIM) * (MLSTM_QK_DIM ** -0.5)
    v = v.astype(F32).reshape(B_, S_, MLSTM_HEADS, MLSTM_V_DIM)
    logi = gates[..., :MLSTM_HEADS]
    logf = jax.nn.log_sigmoid(gates[..., MLSTM_HEADS:])
    hs = mlstm_chunkwise(q, k, v, logi, logf)
    hs = rms_norm_f32(hs, h_gain.reshape(MLSTM_HEADS, MLSTM_V_DIM))
    y = hs.reshape(B_, S_, v_w) * jax.nn.sigmoid(og.astype(F32))
    return y.astype(h.dtype) @ w_out

def hierarchical_moe(h, w_group, b_group, w_expert, b_expert, w_gate, w_up, w_down):
    B_, S_, D_ = h.shape
    N = B_ * S_
    xf = h.reshape(N, D_)
    g_logits = (xf @ w_group).astype(F32) + b_group.astype(F32)
    g_prob = jax.nn.softmax(g_logits, axis=-1)
    _, grp = lax.top_k(g_logits, 1)
    grp = grp[:, 0]
    p_grp = jnp.take_along_axis(g_prob, grp[:, None], axis=-1)[:, 0]
    e_logits = ((xf @ w_expert).astype(F32) + b_expert.astype(F32)).reshape(N, N_GROUPS, EXPERTS_PER_GROUP)
    e_in = jnp.take_along_axis(e_logits, grp[:, None, None], axis=1)[:, 0]
    top_v, top_i = lax.top_k(e_in, TOP_K_IN_GROUP)
    gates = p_grp[:, None] * jax.nn.softmax(top_v, axis=-1)
    expert_id = grp[:, None] * EXPERTS_PER_GROUP + top_i

    A = N * TOP_K_IN_GROUP
    e_flat = expert_id.reshape(A).astype(jnp.int32)
    tok_flat = jnp.repeat(jnp.arange(N, dtype=jnp.int32), TOP_K_IN_GROUP)
    g_flat = gates.reshape(A)
    order = jnp.argsort(e_flat)
    e_s, tok_s, g_s = e_flat[order], tok_flat[order], g_flat[order]
    counts = jnp.bincount(e_flat, length=N_EXPERTS)
    padded = ((counts + MOE_BLOCK - 1) // MOE_BLOCK) * MOE_BLOCK
    pad_end = jnp.cumsum(padded)
    pad_start = pad_end - padded
    start = jnp.cumsum(counts) - counts
    dest = pad_start[e_s] + jnp.arange(A, dtype=jnp.int32) - start[e_s]
    P = (A // MOE_BLOCK + N_EXPERTS) * MOE_BLOCK
    nb = P // MOE_BLOCK
    row_tok = jnp.full((P,), N, dtype=jnp.int32).at[dest].set(tok_s)
    row_gate = jnp.zeros((P,), F32).at[dest].set(g_s)
    block_exp = jnp.clip(jnp.searchsorted(pad_end, jnp.arange(nb) * MOE_BLOCK, side='right'), 0, N_EXPERTS - 1)
    x_pad = jnp.concatenate([xf, jnp.zeros((1, D_), xf.dtype)], axis=0)
    xs = x_pad[row_tok].reshape(nb, MOE_BLOCK, D_)

    def expert_block(args):
        xb, e = args
        return (jax.nn.silu(xb @ w_gate[e]) * (xb @ w_up[e])) @ w_down[e]

    ys = lax.map(expert_block, (xs, block_exp)).reshape(P, D_)
    out = jnp.zeros((N + 1, D_), F32).at[row_tok].add(ys.astype(F32) * row_gate[:, None])[:N]
    return out.reshape(B_, S_, D_).astype(h.dtype)

def setup_inputs(seed: int = 0) -> dict:
    key = jax.random.key(seed)
    ks = jax.random.split(key, 24)
    n_attn = (DEPTH + N_MIXERS - 1) // N_MIXERS
    n_mlstm = DEPTH // N_MIXERS
    d = D_MODEL
    attn_w = ATTN_HEADS * ATTN_HEAD_DIM
    qk_w = MLSTM_HEADS * MLSTM_QK_DIM
    v_w = MLSTM_HEADS * MLSTM_V_DIM
    nrm = jax.random.normal
    return {
        "x": nrm(ks[0], (BATCH, SEQ, d), F32),
        "norm_mix": 1.0 + 0.02 * nrm(ks[1], (DEPTH, d), F32),
        "norm_ffn": 1.0 + 0.02 * nrm(ks[2], (DEPTH, d), F32),
        "attn_w_in": nrm(ks[3], (n_attn, d, 3 * attn_w), F32) * d ** -0.5,
        "attn_q_norm": 1.0 + 0.02 * nrm(ks[4], (n_attn, ATTN_HEAD_DIM), F32),
        "attn_k_norm": 1.0 + 0.02 * nrm(ks[5], (n_attn, ATTN_HEAD_DIM), F32),
        "attn_w_out": nrm(ks[6], (n_attn, attn_w, d), F32) * attn_w ** -0.5,
        "mlstm_w_in": nrm(ks[7], (n_mlstm, d, 2 * qk_w + 2 * v_w + 2 * MLSTM_HEADS), F32) * d ** -0.5,
        "mlstm_conv_w": nrm(ks[8], (n_mlstm, CONV_WIDTH, 2 * qk_w), F32) * CONV_WIDTH ** -0.5,
        "mlstm_conv_b": 0.02 * nrm(ks[9], (n_mlstm, 2 * qk_w), F32),
        "mlstm_gate_b": jnp.concatenate([
            0.1 * nrm(ks[10], (n_mlstm, MLSTM_HEADS), F32),
            jax.random.uniform(ks[11], (n_mlstm, MLSTM_HEADS), F32, 3.0, 6.0)], axis=-1),
        "mlstm_h_norm": 1.0 + 0.02 * nrm(ks[12], (n_mlstm, v_w), F32),
        "mlstm_w_out": nrm(ks[13], (n_mlstm, v_w, d), F32) * v_w ** -0.5,
        "moe_w_group": nrm(ks[14], (DEPTH, d, N_GROUPS), F32) * d ** -0.5,
        "moe_b_group": 0.01 * nrm(ks[15], (DEPTH, N_GROUPS), F32),
        "moe_w_expert": nrm(ks[16], (DEPTH, d, N_EXPERTS), F32) * d ** -0.5,
        "moe_b_expert": 0.01 * nrm(ks[17], (DEPTH, N_EXPERTS), F32),
        "moe_w_gate": nrm(ks[18], (DEPTH, N_EXPERTS, d, EXPERT_FF), F32) * d ** -0.5,
        "moe_w_up": nrm(ks[19], (DEPTH, N_EXPERTS, d, EXPERT_FF), F32) * d ** -0.5,
        "moe_w_down": nrm(ks[20], (DEPTH, N_EXPERTS, EXPERT_FF, d), F32) * EXPERT_FF ** -0.5,
    }

def reference(x, norm_mix, norm_ffn, attn_w_in, attn_q_norm, attn_k_norm, attn_w_out,
              mlstm_w_in, mlstm_conv_w, mlstm_conv_b, mlstm_gate_b, mlstm_h_norm, mlstm_w_out,
              moe_w_group, moe_b_group, moe_w_expert, moe_b_expert, moe_w_gate, moe_w_up, moe_w_down):
    for layer in range(DEPTH):
        j = layer // N_MIXERS
        h = rms_norm(x, norm_mix[layer])
        if layer % N_MIXERS == 0:
            x = x + dilated_attention_mixer(h, attn_w_in[j], attn_q_norm[j], attn_k_norm[j], attn_w_out[j])
        else:
            x = x + mlstm_mixer(h, mlstm_w_in[j], mlstm_conv_w[j], mlstm_conv_b[j], mlstm_gate_b[j],
                                mlstm_h_norm[j], mlstm_w_out[j])
        h = rms_norm(x, norm_ffn[layer])
        x = x + hierarchical_moe(h, moe_w_group[layer], moe_b_group[layer], moe_w_expert[layer],
                                 moe_b_expert[layer], moe_w_gate[layer], moe_w_up[layer], moe_w_down[layer])
    return x


_drawn_inputs = setup_inputs


def setup_inputs(seed=0):
    import zlib

    import numpy as np

    out = dict(_drawn_inputs(seed))
    spreads = {}
    factors = {'norm_mix': 4.462,
     'norm_ffn': 2.885,
     'attn_q_norm': 7.198,
     'attn_k_norm': 5.731,
     'moe_b_group': 8.0,
     'moe_b_expert': 5.911}
    for name, (base, spread) in spreads.items():
        noise = np.random.default_rng([zlib.crc32(name.encode()), seed]).standard_normal(out[name].shape)
        drawn = base * np.exp(spread * noise) if base else spread * noise
        out[name] = __import__('jax').numpy.asarray(drawn.astype(out[name].dtype))
    for name, factor in factors.items():
        out[name] = (out[name] * factor).astype(out[name].dtype)
    return out
```

```python
from contextlib import ExitStack

import numpy as np

import concourse.bass as bass
from concourse import mybir

F32 = mybir.dt.float32
BF16 = mybir.dt.bfloat16
I32 = mybir.dt.int32
ACT = mybir.ActivationFunctionType
ALU = mybir.AluOpType
AX = mybir.AxisListType

P = 128
SEQ, D = 512, 1024
TILES = SEQ // P
CHUNKS = D // P
HEADS, DH = 16, 64
PAIRS = HEADS // 2
BRANCHES = ((128, 1), (512, 4), (2048, 16))
EPS = 1e-6
GROUPS, PER_GROUP = 8, 8
EXPERTS = GROUPS * PER_GROUP
FF = D // 2
FQ = FF // P
SLOTS = 32
SET = P // SLOTS
MAX_ROUNDS = SEQ // SLOTS
NEVER = -1.0e30
PIECE = 4096
RING = 6
W_OUT_PIECE = 3

_WIDTHS = dict(ident=P, logmult=SEQ, gain_mix=CHUNKS, gain_ffn_gather=CHUNKS, gain_ffn_router=CHUNKS, q_gain=1,
               k_gain=1, eps=1, bias=GROUPS + EXPERTS, first8=GROUPS, first64=EXPERTS, slot=SLOTS,
               round_start=MAX_ROUNDS, earlier=P, router=CHUNKS * P)
COLS, _at = {}, 0
for _name, _w in _WIDTHS.items():
    COLS[_name] = (_at, _at + _w)
    _at += _w
PARAMS = _at


def constants():
    d = (SEQ - P) + np.arange(P)[:, None] - np.arange(SEQ)[None, :]
    times = sum(((d >= 0) & (d % dil == 0) & (d <= win)).astype(np.float64) for win, dil in BRANCHES)
    return dict(
        ident=np.eye(P),
        logmult=np.where(times > 0, np.log(np.maximum(times, 1)), NEVER),
        eps=np.full((P, 1), EPS),
        first8=np.tile(GROUPS - np.arange(GROUPS), (P, 1)),
        first64=np.tile(EXPERTS - np.arange(EXPERTS), (P, 1)),
        slot=np.tile(np.arange(SLOTS), (P, 1)),
        round_start=np.tile(SLOTS * np.arange(MAX_ROUNDS), (P, 1)),
        earlier=np.triu(np.ones((P, P)), 1),
    )


def trunk(nc, x, params, w_in, w_out, w_gate, w_up, w_down, out):
    ctx = ExitStack()
    with ctx:
        def sem(name):
            return ctx.enter_context(nc.semaphore(name))

        REGION = 4096
        SMALL = PARAMS + 3 * 512 + 280
        arena = ctx.enter_context(nc.sbuf_tensor("arena", [P, 12 * REGION + SMALL], F32))
        taken = [0]

        def take(n):
            taken[0] += n
            return arena[:, taken[0] - n:taken[0]]

        ring = take(RING * PIECE).rearrange("p (s n) -> p s n", s=RING)
        resid = take(REGION).rearrange("p (t n) -> p t n", t=TILES)
        region_h = take(REGION)
        region_q = take(REGION)
        region_k = take(2 * REGION)
        region_v = take(REGION)
        par_sb = take(PARAMS)
        qk_norm = take(2 * 512).rearrange("p (b n) -> p b n", b=2)
        squares = take(512)
        unused_squares = arena[:, taken[0] - 1024:taken[0]]
        small_at = taken[0]

        def const(name):
            a, b = COLS[name]
            return par_sb[:, a:b]

        ident = const("ident")
        router = const("router").rearrange("p (c n) -> p c n", c=CHUNKS)

        hT = region_h.rearrange("p (c s) -> p c s", c=CHUNKS)
        xn = region_v.rearrange("p (t n) -> p t n", t=TILES)
        qT = region_q.rearrange("p (m s) -> p m s", m=PAIRS)
        kTz = region_k.rearrange("p (z m s) -> p z m s", z=2, m=PAIRS)
        v = region_v.rearrange("p (t n) -> p t n", t=TILES)
        N_PROB = 6
        prob = region_h[:, 0:N_PROB * 512].rearrange("p (b n) -> p b n", b=N_PROB)
        probT = region_h[:, N_PROB * 512:REGION].rearrange("p (b n) -> p b n", b=2)
        w_out_sb = ring[:, W_OUT_PIECE:W_OUT_PIECE + 2, :].rearrange("p s n -> p (s n)").rearrange(
            "p (c n) -> p c n", c=CHUNKS)

        h2 = region_h.rearrange("p (t k d) -> p t k d", t=TILES, k=CHUNKS)
        xT = region_k.rearrange("p (b k s) -> p b k s", b=8, k=CHUNKS)[:, 0:2]
        y_rows = region_k.rearrange("p (b n) -> p b n", b=8)[:, 2:4, :]
        pick = region_k.rearrange("p (b t s) -> p b t s", b=16, t=TILES)[:, 8:10]
        pick_gated = region_k.rearrange("p (b t s) -> p b t s", b=16, t=TILES)[:, 10:12]
        spread = region_k.rearrange("p (b t s) -> p b t s", b=16, t=TILES)[:, 12:14]
        hidden_gate = region_k[:, 14 * 512:14 * 512 + P]
        hidden = region_k[:, 14 * 512 + P:14 * 512 + 2 * P]
        hiddenT = region_k[:, 14 * 512 + 2 * P:14 * 512 + 3 * P]

        rt = [0]

        def rview(*shape):
            n = int(np.prod(shape))
            a = region_v[:, rt[0]:rt[0] + n]
            rt[0] += n
            if len(shape) == 2:
                a = a.rearrange("p (a b) -> p a b", a=shape[0])
            return a

        logits = qk_norm[:, 0, 0:TILES * (GROUPS + EXPERTS)].rearrange("p (t n) -> p t n", t=TILES)
        scaled = rview(TILES, GROUPS + EXPERTS)
        group_top = rview(TILES)
        group_low = rview(TILES, GROUPS)
        group_exp = rview(TILES, GROUPS)
        group_sum = rview(TILES)
        group_prob = rview(TILES)
        group_is = rview(TILES, GROUPS)
        group_val = rview(TILES, GROUPS)
        group_first = rview(TILES)
        cand = rview(TILES, EXPERTS)
        is_top = rview(TILES, EXPERTS)
        top_val = rview(TILES, EXPERTS)
        top = [rview(TILES), rview(TILES)]
        first = [rview(TILES), rview(TILES)]
        chosen = [rview(TILES, EXPERTS), rview(TILES, EXPERTS)]
        gap = rview(TILES)
        ratio = rview(TILES)
        denom = rview(TILES)
        inv = rview(TILES)
        gate = [rview(TILES), rview(TILES)]
        gated = rview(TILES, EXPERTS)
        AHEAD = 2 * SET
        rank = rview(TILES, EXPERTS + AHEAD)
        weight = rview(TILES, EXPERTS + AHEAD)
        picked = rview(TILES * EXPERTS // 2).bitcast(BF16).rearrange("p (t e) -> p t e", t=TILES)
        ranked = rview(TILES, EXPERTS)
        fullest = rview(1)
        is_round = rview(MAX_ROUNDS)
        rounds_f = rview(1)
        slot_now = rview(SLOTS)
        counts_i = ctx.enter_context(nc.sbuf_tensor("counts_i", [P, 2], I32))
        earlier_bf = ctx.enter_context(nc.sbuf_tensor("earlier_bf", [P, P], BF16))
        ones_bf = ctx.enter_context(nc.sbuf_tensor("ones_bf", [P, P], BF16))

        def small(n):
            return take(n)

        ssq = small(TILES)
        std = small(TILES)
        rstd = small(TILES)
        ssq2 = small(TILES)
        std2 = small(TILES)
        rstd2 = small(TILES)
        head_ssq = small(16).rearrange("p (b n) -> p b n", b=2)
        head_std = small(16).rearrange("p (b n) -> p b n", b=2)
        head_rstd = small(16).rearrange("p (b n) -> p b n", b=2)
        qk_scale = small(1)
        neg_max = small(TILES * HEADS)
        row_sum = small(TILES * HEADS)
        row_inv = small(TILES * HEADS)
        assert taken[0] <= 12 * REGION + SMALL, taken[0]

        bank = [ctx.enter_context(nc.psum_tensor(f"bank{i}", [P, 512], F32)) for i in range(8)]

        x_in = [sem(f"x_in{t}") for t in range(TILES)]
        params_in = sem("params_in")
        ring_in = [sem(f"ring_in{s}") for s in range(RING)]
        tables_ready = sem("tables_ready")
        pool_step = sem("pool_step")
        qk_scale_ready = sem("qk_scale_ready")
        ssq_done = sem("ssq_done")
        std_done = sem("std_done")
        rstd_done = sem("rstd_done")
        xn_done = sem("xn_done")
        xnT_done = sem("xnT_done")
        hT_done = sem("hT_done")
        proj_done = sem("proj_done")
        sq_done = sem("sq_done")
        hssq_done = sem("hssq_done")
        hstd_done = sem("hstd_done")
        hrstd_done = sem("hrstd_done")
        qk_normed = sem("qk_normed")
        qkT_psum = sem("qkT_psum")
        qkT_done = sem("qkT_done")
        v_done = sem("v_done")
        score_done = sem("score_done")
        masked_done = sem("masked_done")
        exp_done = sem("exp_done")
        inv_done = sem("inv_done")
        prob_done = sem("prob_done")
        probT_psum = sem("probT_psum")
        probT_done = [sem("probT_done_even"), sem("probT_done_odd")]
        attn_psum = sem("attn_psum")
        attn_done = sem("attn_done")
        mix_psum = sem("mix_psum")
        mix_done = sem("mix_done")
        ssq2_done = sem("ssq2_done")
        x2T_psum = sem("x2T_psum")
        x2T_done = sem("x2T_done")
        logit_psum = sem("logit_psum")
        logit_done = sem("logit_done")
        rt_dve = sem("rt_dve")
        std2_done = sem("std2_done")
        rstd2_ready = sem("rstd2_ready")
        low_ready = sem("low_ready")
        gexp_done = sem("gexp_done")
        gap_ready = sem("gap_ready")
        ratio_done = sem("ratio_done")
        picked_ready = sem("picked_ready")
        rank_psum = sem("rank_psum")
        routing_done = sem("routing_done")
        h2_done = sem("h2_done")
        slot_ready = sem("slot_ready")
        pick_done = sem("pick_done")
        pickg_done = sem("pickg_done")
        gather_psum = sem("gather_psum")
        xT_done = sem("xT_done")
        up_psum = sem("up_psum")
        silu_done = sem("silu_done")
        hidden_done = sem("hidden_done")
        hiddenT_psum = sem("hiddenT_psum")
        hiddenT_done = sem("hiddenT_done")
        spread_psum = sem("spread_psum")
        spread_done = sem("spread_done")
        down_psum = sem("down_psum")
        y_done_act = sem("y_done_act")
        y_done_dve = sem("y_done_dve")
        combine_psum = sem("combine_psum")
        added = sem("added")
        out_stored = sem("out_stored")

        BLOCKS = 6
        QK_UNITS = 4 * TILES
        UNITS = TILES * PAIRS
        ITER = 2 * SET
        ITERS = EXPERTS // ITER

        def keys(n):
            return (n // PAIRS + 1) * P

        gate_v = w_gate.rearrange("e (p k) n -> e p (k n)", k=CHUNKS)
        up_v = w_up.rearrange("e (p k) n -> e p (k n)", k=CHUNKS)
        down_v = w_down.rearrange("e (j p) n -> e p j n", p=P)
        before = [2 if s in (W_OUT_PIECE, W_OUT_PIECE + 1) else 1 for s in range(RING)]

        def loaded(s, use):
            return (use + 1 + before[s]) * 16

        block = ctx.enter_context(nc.Block())

        @block.sync
        def _(sp):
            for t in range(TILES):
                sp.dma_start(resid[:, t, :], x[t * P:(t + 1) * P, :]).then_inc(x_in[t], 16)
                if t == 0:
                    sp.dma_start(par_sb, params).then_inc(params_in, 16)
            for b in range(BLOCKS):
                sp.dma_start(ring[:, b, :].rearrange("p (c n) -> p c n", c=CHUNKS),
                             w_in[:, b * 512:(b + 1) * 512].rearrange("(c p) n -> p c n", p=P)
                             ).then_inc(ring_in[b], 16)

            def load_down(s, e):
                sp.dma_start(ring[:, s, :].rearrange("p (j n) -> p j n", j=FQ), down_v[e]).then_inc(ring_in[s], 16)

            sp.wait_ge(proj_done, TILES * 1)
            sp.dma_start(ring[:, 0, :], gate_v[0]).then_inc(ring_in[0], 16)
            sp.wait_ge(proj_done, TILES * 2)
            sp.dma_start(ring[:, 1, :], up_v[0]).then_inc(ring_in[1], 16)
            sp.wait_ge(proj_done, TILES * 3)
            load_down(2, 0)
            sp.wait_ge(proj_done, TILES * 5)
            for s in range(2):
                sp.dma_start(w_out_sb[:, s * FQ:(s + 1) * FQ, :],
                             w_out[s * 512:(s + 1) * 512, :].rearrange("(c p) n -> p c n", p=P)
                             ).then_inc(ring_in[W_OUT_PIECE + s], 16)
            sp.wait_ge(proj_done, TILES * 6)
            load_down(5, 1)
            sp.wait_ge(mix_psum, 2 * TILES)
            sp.dma_start(ring[:, 3, :], gate_v[1]).then_inc(ring_in[3], 16)
            sp.dma_start(ring[:, 4, :], up_v[1]).then_inc(ring_in[4], 16)

            def load_pair(expert, done):
                for u in range(2):
                    sp.wait_ge(up_psum, done + u + 1)
                    sp.dma_start(ring[:, 3 * u, :], gate_v[expert + u]).then_inc(ring_in[3 * u], 16)
                    sp.dma_start(ring[:, 3 * u + 1, :], up_v[expert + u]).then_inc(ring_in[3 * u + 1], 16)
                    sp.wait_ge(down_psum, done + u + 1)
                    load_down(3 * u + 2, expert + u)

            with sp.Fori(1, EXPERTS // 2) as j:
                load_pair(j * 2, j * 2 - 2)
            sp.wait_ge(routing_done, 1)
            rounds = sp.value_load(counts_i[0:1, 1:2], min_val=1, max_val=MAX_ROUNDS)
            with sp.If(rounds > 1):
                with sp.Fori(1, rounds) as r:
                    with sp.Fori(0, EXPERTS // 2) as j:
                        load_pair(j * 2, r * EXPERTS + j * 2 - 2)
            for t in range(TILES):
                sp.wait_ge(added, rounds * (2 * EXPERTS) + (2 * t + 3))
                sp.dma_start(out[t * P:(t + 1) * P, :], resid[:, t, :]).then_inc(out_stored, 16)
            sp.wait_ge(out_stored, 16 * TILES)

        @block.tensor
        def _(pe):
            mm, tr = nc.tensor.matmul, nc.tensor.transpose
            pe.wait_ge(params_in, 16)

            for t in range(TILES):
                pe.wait_ge(xn_done, t + 1)
                for half in range(2):
                    b = 4 + (2 * t + half) % 4
                    if t >= 2:
                        pe.wait_ge(hT_done, 2 * (t - 2) + half + 1)
                    for c in range(4):
                        last = tr(bank[b][:, c * P:(c + 1) * P],
                                  xn[:, t, (4 * half + c) * P:(4 * half + c + 1) * P], ident)
                    last.then_inc(xnT_done, 1)

            def project(u):
                b, t = divmod(u, TILES)
                if t == 0:
                    pe.wait_ge(ring_in[b], 16)
                if u < TILES:
                    pe.wait_ge(hT_done, 2 * (t + 1))
                if u >= 2:
                    if u - 2 < QK_UNITS:
                        pe.wait_ge(qk_normed, u - 1)
                    else:
                        pe.wait_ge(v_done, u - 1 - QK_UNITS)
                for c in range(CHUNKS):
                    last = mm(bank[u % 2][:, :], hT[:, c, t * P:(t + 1) * P], ring[:, b, c * 512:(c + 1) * 512],
                              start=(c == 0), stop=(c == CHUNKS - 1))
                last.then_inc(proj_done, 1)

            def turn_qk(u):
                pe.wait_ge(qk_normed, u + 1)
                if u >= 2:
                    pe.wait_ge(qkT_done, u - 1)
                for c in range(4):
                    last = tr(bank[2 + u % 2][:, c * P:(c + 1) * P], qk_norm[:, u % 2, c * P:(c + 1) * P], ident)
                last.then_inc(qkT_psum, 1)

            for u in range(BLOCKS * TILES):
                project(u)
                if 1 <= u <= QK_UNITS:
                    turn_qk(u - 1)

            def scores(n):
                i, m = divmod(n, PAIRS)
                if n == 0:
                    pe.wait_ge(qkT_done, QK_UNITS)
                    pe.wait_ge(v_done, 2 * TILES)
                for z in range(2):
                    if n >= 2:
                        pe.wait_ge(masked_done, 2 * (n - 2) + z + 1)
                    mm(bank[2 * (n % 2) + z][:, 0:keys(n)], qT[:, m, i * P:(i + 1) * P], kTz[:, z, m, 0:keys(n)],
                       start=True, stop=True).then_inc(score_done, 1)

            def turn_probs(n):
                for z in range(2):
                    pe.wait_ge(prob_done, 2 * n + z + 1)
                    if n >= 1:
                        pe.wait_ge(probT_done[z], n)
                    for kb in range(n // PAIRS + 1):
                        last = tr(bank[4 + z][:, kb * P:(kb + 1) * P],
                                  prob[:, (2 * n + z) % N_PROB, kb * P:(kb + 1) * P], ident)
                    last.then_inc(probT_psum, 1)

            def attend(n):
                i, m = divmod(n, PAIRS)
                pe.wait_ge(probT_done[0], n + 1)
                pe.wait_ge(probT_done[1], n + 1)
                if n >= 1:
                    pe.wait_ge(attn_done, n)
                for kb in range(i + 1):
                    for z in range(2):
                        last = mm(bank[6][z * DH:(z + 1) * DH, 0:P],
                                  v[:, kb, (2 * m + z) * DH:(2 * m + z + 1) * DH],
                                  probT[:, z, kb * P:(kb + 1) * P],
                                  start=(kb == 0), stop=(kb == i))
                last.then_inc(attn_psum, 1)

            def mix(i, half):
                if half == 0:
                    pe.wait_ge(attn_done, PAIRS * (i + 1))
                if i == 0 and half == 0:
                    pe.wait_ge(ring_in[W_OUT_PIECE], 32)
                    pe.wait_ge(ring_in[W_OUT_PIECE + 1], 32)
                if half == 1:
                    pe.wait_ge(mix_done, 2 * i + 1)
                elif i >= 1:
                    pe.wait_ge(logit_done, i)
                for c in range(CHUNKS):
                    last = mm(bank[7][:, :], qT[:, c, i * P:(i + 1) * P], w_out_sb[:, c, half * 512:(half + 1) * 512],
                              start=(c == 0), stop=(c == CHUNKS - 1))
                last.then_inc(mix_psum, 1)

            def turn_x2(i, half):
                pe.wait_ge(mix_done, 2 * (i + 1))
                if half == 1:
                    pe.wait_ge(x2T_done, 2 * i + 1)
                for c in range(4):
                    last = tr(bank[7][:, c * P:(c + 1) * P],
                              resid[:, i, (4 * half + c) * P:(4 * half + c + 1) * P], ident)
                last.then_inc(x2T_psum, 1)

            def route(i):
                pe.wait_ge(x2T_done, 2 * (i + 1))
                pe.wait_ge(tables_ready, 1)
                for c in range(CHUNKS):
                    last = mm(bank[7][:, 0:P], qT[:, c, i * P:(i + 1) * P], router[:, c, :],
                              start=(c == 0), stop=(c == CHUNKS - 1))
                last.then_inc(logit_psum, 1)

            def tail(i, step):
                (lambda: mix(i, 0), lambda: mix(i, 1), lambda: turn_x2(i, 0), lambda: turn_x2(i, 1),
                 lambda: route(i))[step]()

            LAG = 3
            for n in range(UNITS + LAG):
                if n < UNITS:
                    scores(n)
                if n >= LAG:
                    attend(n - LAG)
                if 2 <= n < UNITS + 2:
                    turn_probs(n - 2)
                i, step = divmod(n - LAG - PAIRS, PAIRS)
                if i >= 0 and step < 5:
                    tail(i, step)
            for step in range(5):
                tail(TILES - 1, step)

            pe.wait_ge(picked_ready, 1)
            pe.wait_ge(tables_ready, 1)
            for t in range(TILES):
                for s in range(t + 1):
                    mm(bank[0][:, t * EXPERTS:(t + 1) * EXPERTS], earlier_bf[:, :] if s == t else ones_bf[:, :],
                       picked[:, s, :], start=(s == 0), stop=(s == t))
            for t in range(TILES):
                last = mm(bank[1][:, 0:EXPERTS], ones_bf[:, :], picked[:, t, :], start=(t == 0), stop=(t == TILES - 1))
            last.then_inc(rank_psum, 1)

            def gather(part, picks):
                b = part % 2
                for c in range(2):
                    for t in range(TILES):
                        last = mm(bank[b][:, c * P:(c + 1) * P], h2[:, t, 2 * part + c, :],
                                  picks[:, t, :], start=(t == 0), stop=(t == TILES - 1))
                last.then_inc(gather_psum, 1)

            def combine(t, half, b):
                return mm(bank[7][:, :], spread[:, b, t, :], y_rows[:, b, half * 512:(half + 1) * 512],
                          start=True, stop=True).then_inc(combine_psum, 1)

            pe.wait_ge(routing_done, 1)
            passes = pe.value_load(counts_i[0:1, 0:1], min_val=ITERS, max_val=ITERS * MAX_ROUNDS)
            pe.wait_ge(h2_done, TILES)
            pe.wait_ge(pick_done, 1)
            for part in range(4):
                if part >= 2:
                    pe.wait_ge(xT_done, part - 1)
                gather(part, pick[:, 0])
            with pe.Fori(0, passes) as it:
                for u in range(ITER):
                    b, e = divmod(u, SET)
                    done = it * ITER + u
                    sets = it * 2 + b
                    s = 3 * (u % 2)
                    use = it * (ITER // 2) + u // 2
                    if e == 0:
                        pe.wait_ge(xT_done, done + SET)
                    pe.wait_ge(ring_in[s], (use + (1 + before[s])) * 16)
                    pe.wait_ge(ring_in[s + 1], (use + (1 + before[s + 1])) * 16)
                    for k in range(CHUNKS):
                        for j in range(FQ):
                            last = mm(bank[2 + u % 2][SLOTS * j:SLOTS * (j + 1), 0:2 * P],
                                      xT[:, b, k, SLOTS * e:SLOTS * (e + 1)],
                                      ring[:, s:s + 2, k * FF + j * P:k * FF + (j + 1) * P],
                                      start=(k == 0), stop=(k == CHUNKS - 1))
                    last.then_inc(up_psum, 1)
                    if e == 0:
                        pe.wait_ge(y_done_act, done + 1)
                        pe.wait_ge(y_done_dve, done + 1)
                        pe.wait_ge(spread_done, sets + 1)
                    for half in range(2):
                        pe.wait_ge(added, done * 2 + (half + 1))
                        combine(e, half, 1 - b)
                    pe.wait_ge(hidden_done, done + 1)
                    tr(bank[4][:, 0:P], hidden, ident).then_inc(hiddenT_psum, 1)
                    if e == 1:
                        pe.wait_ge(pickg_done, sets + 1)
                        for t in range(TILES):
                            last = tr(bank[5][:, t * P:(t + 1) * P], pick_gated[:, b, t, :], ident)
                        last.then_inc(spread_psum, 1)
                    if e == 0:
                        pe.wait_ge(pick_done, sets + 2)
                    pe.wait_ge(xT_done, done + 3)
                    gather(e, pick[:, 1 - b])
                    pe.wait_ge(hiddenT_done, done + 1)
                    pe.wait_ge(ring_in[s + 2], (use + (1 + before[s + 2])) * 16)
                    pe.wait_ge(y_done_act, done + 1)
                    pe.wait_ge(y_done_dve, done + 1)
                    for j in range(FQ):
                        for q in range(4):
                            last = mm(bank[6][SLOTS * q:SLOTS * (q + 1), 0:256], hiddenT[:, SLOTS * j:SLOTS * (j + 1)],
                                      ring[:, s + 2, j * D + q * 256:j * D + (q + 1) * 256],
                                      start=(j == 0), stop=(j == FQ - 1))
                    last.then_inc(down_psum, 1)
            pe.wait_ge(y_done_act, passes * ITER + 1)
            pe.wait_ge(y_done_dve, passes * ITER + 1)
            pe.wait_ge(spread_done, passes * 2 + 1)
            for t in range(TILES):
                for half in range(2):
                    pe.wait_ge(added, passes * (2 * ITER) + (2 * t + half + 1))
                    combine(t, half, 1)

        @block.scalar
        def _(act):
            fn = nc.scalar.activation
            act.wait_ge(params_in, 16)
            for t in range(TILES):
                act.wait_ge(x_in[t], 16)
                fn(region_q[:, t * D:(t + 1) * D], resid[:, t, :], ACT.Square,
                   accum_out=ssq[:, t:t + 1]).then_inc(ssq_done, 1)
                act.wait_ge(ssq_done, t + 1)
                fn(std[:, t:t + 1], ssq[:, t:t + 1], ACT.Sqrt, bias=const("eps"), scale=1.0 / D).then_inc(std_done, 1)

            def store_qk(u):
                b, t = divmod(u, TILES)
                act.wait_ge(qkT_psum, u + 1)
                src = bank[2 + u % 2][:, :].rearrange("p (m s) -> p m s", m=4)
                pairs, toks = slice(4 * (b % 2), 4 * (b % 2) + 4), slice(t * P, (t + 1) * P)
                if b < 2:
                    fn(qT[:, pairs, toks], src, ACT.Copy, scale=qk_scale).then_inc(qkT_done, 1)
                else:
                    fn(kTz[0:DH, 0, pairs, toks], src[0:DH], ACT.Copy)
                    fn(kTz[DH:P, 1, pairs, toks], src[DH:P], ACT.Copy).then_inc(qkT_done, 1)

            act.wait_ge(qk_scale_ready, 1)
            act.wait_ge(tables_ready, 1)
            for u in range(QK_UNITS):
                act.wait_ge(proj_done, u + 1)
                if u >= 1:
                    act.wait_ge(hssq_done, u)
                fn(squares, bank[u % 2][:, :], ACT.Square).then_inc(sq_done, 1)
                act.wait_ge(hssq_done, u + 1)
                fn(head_std[:, u % 2, :], head_ssq[:, u % 2, :], ACT.Sqrt, bias=const("eps"),
                   scale=1.0 / DH).then_inc(hstd_done, 1)
                if u >= 1:
                    store_qk(u - 1)
            for u in range(2 * TILES):
                b, t = divmod(u, TILES)
                act.wait_ge(proj_done, QK_UNITS + u + 1)
                fn(v[:, t, b * 512:(b + 1) * 512], bank[u % 2][:, :], ACT.Copy).then_inc(v_done, 1)
                if u == 0:
                    store_qk(QK_UNITS - 1)

            def exponent(n):
                for z in range(2):
                    h, w = 2 * n + z, keys(n)
                    act.wait_ge(masked_done, h + 1)
                    fn(prob[:, h % N_PROB, 0:w], prob[:, h % N_PROB, 0:w], ACT.Exp, scale=-1.0,
                       bias=neg_max[:, h:h + 1], accum_out=row_sum[:, h:h + 1]).then_inc(exp_done, 1)

            def store_probT(n):
                act.wait_ge(probT_psum, 2 * n + 2)
                if n >= 1:
                    act.wait_ge(attn_psum, n)
                fn(probT[:, 1, 0:keys(n)], bank[5][:, 0:keys(n)], ACT.Copy).then_inc(probT_done[1], 1)

            def store_attn(n):
                i, m = divmod(n, PAIRS)
                act.wait_ge(attn_psum, n + 1)
                fn(qT[:, m, i * P:(i + 1) * P], bank[6][:, 0:P], ACT.Copy).then_inc(attn_done, 1)

            def store_x2T(i, half):
                act.wait_ge(x2T_psum, 2 * i + half + 1)
                fn(qT[:, 4 * half:4 * half + 4, i * P:(i + 1) * P],
                   bank[7][:, :].rearrange("p (c s) -> p c s", c=4), ACT.Copy).then_inc(x2T_done, 1)

            def square_x2(i):
                act.wait_ge(mix_done, 2 * (i + 1))
                fn(unused_squares, resid[:, i, :],
                   ACT.Square, accum_out=ssq2[:, i:i + 1]).then_inc(ssq2_done, 1)

            LAG = 3
            for n in range(UNITS + LAG):
                if n < UNITS:
                    exponent(n)
                if n >= LAG:
                    store_attn(n - LAG)
                if 2 <= n < UNITS + 2:
                    store_probT(n - 2)
                i, step = divmod(n - LAG - PAIRS, PAIRS)
                if i >= 0 and step in (2, 3):
                    store_x2T(i, step - 2)
                if i >= 0 and step == 4:
                    square_x2(i)
            square_x2(TILES - 1)
            act.wait_ge(ssq2_done, TILES)
            fn(std2, ssq2, ACT.Sqrt, bias=const("eps"), scale=1.0 / D).then_inc(std2_done, 1)
            store_x2T(TILES - 1, 0)
            store_x2T(TILES - 1, 1)

            act.wait_ge(low_ready, 1)
            fn(group_exp, group_low, ACT.Exp).then_inc(gexp_done, 1)
            act.wait_ge(gap_ready, 1)
            fn(ratio, gap, ACT.Exp).then_inc(ratio_done, 1)

            act.wait_ge(routing_done, 1)
            passes = act.value_load(counts_i[0:1, 0:1], min_val=ITERS, max_val=ITERS * MAX_ROUNDS)
            act.sem_inc(y_done_act, 1)
            with act.Fori(0, passes) as it:
                for u in range(ITER):
                    b, e = divmod(u, SET)
                    done = it * ITER + u
                    sets = it * 2 + b
                    act.wait_ge(up_psum, done + 1)
                    fn(hidden_gate, bank[2 + u % 2][:, 0:P], ACT.Silu).then_inc(silu_done, 1)
                    act.wait_ge(hiddenT_psum, done + 1)
                    fn(hiddenT, bank[4][:, 0:P], ACT.Copy).then_inc(hiddenT_done, 1)
                    if e == 1:
                        act.wait_ge(spread_psum, sets + 1)
                        fn(spread[:, b].rearrange("p t s -> p (t s)"), bank[5][:, :], ACT.Copy
                           ).then_inc(spread_done, 1)
                    act.wait_ge(down_psum, done + 1)
                    for q in range(2):
                        last = fn(y_rows[SLOTS * e:SLOTS * (e + 1), b, q * 256:(q + 1) * 256],
                                  bank[6][SLOTS * q:SLOTS * (q + 1), 0:256], ACT.Copy)
                    last.then_inc(y_done_act, 1)

        @block.vector
        def _(dve):
            ve = nc.vector
            dve.wait_ge(params_in, 16)
            ve.scalar_tensor_tensor(qk_scale, const("q_gain"), DH ** -0.5, const("k_gain"), ALU.mult, ALU.mult
                                    ).then_inc(qk_scale_ready, 1)
            for t in range(TILES):
                dve.wait_ge(std_done, t + 1)
                ve.reciprocal(rstd[:, t:t + 1], std[:, t:t + 1]).then_inc(rstd_done, 1)
                dve.wait_ge(rstd_done, t + 1)
                ve.tensor_scalar(xn[:, t, :], resid[:, t, :], rstd[:, t:t + 1], None, ALU.mult).then_inc(xn_done, 1)
                for half in range(2):
                    dve.wait_ge(xnT_done, 2 * t + half + 1)
                    ve.tensor_tensor(hT[:, 4 * half:4 * half + 4, t * P:(t + 1) * P],
                                     bank[4 + (2 * t + half) % 4][:, :].rearrange("p (c s) -> p c s", c=4),
                                     const("gain_mix")[:, 4 * half:4 * half + 4, None].to_broadcast([P, 4, P]),
                                     ALU.mult).then_inc(hT_done, 1)

            for u in range(QK_UNITS):
                dve.wait_ge(sq_done, u + 1)
                ve.tensor_reduce(head_ssq[:, u % 2, :], squares.rearrange("p (h d) -> p h d", h=8), AX.X, ALU.add
                                 ).then_inc(hssq_done, 1)
                dve.wait_ge(hstd_done, u + 1)
                ve.reciprocal(head_rstd[:, u % 2, :], head_std[:, u % 2, :]).then_inc(hrstd_done, 1)
                dve.wait_ge(hrstd_done, u + 1)
                if u >= 2:
                    dve.wait_ge(qkT_psum, u - 1)
                ve.tensor_tensor(qk_norm[:, u % 2, :].rearrange("p (h d) -> p h d", h=8),
                                 bank[u % 2][:, :].rearrange("p (h d) -> p h d", h=8),
                                 head_rstd[:, u % 2, :, None].to_broadcast([P, 8, DH]), ALU.mult
                                 ).then_inc(qk_normed, 1)

            def mask(n):
                for z in range(2):
                    h, w = 2 * n + z, keys(n)
                    dve.wait_ge(score_done, h + 1)
                    if n >= 3:
                        dve.wait_ge(probT_psum, h - N_PROB + 1)
                    ve.tensor_tensor_reduce(prob[:, h % N_PROB, 0:w], bank[2 * (n % 2) + z][:, 0:w],
                                            const("logmult")[:, SEQ - w:SEQ], -1.0, 3.0e38, ALU.add, ALU.min,
                                            neg_max[:, h:h + 1]).then_inc(masked_done, 1)

            def invert(n):
                dve.wait_ge(exp_done, 2 * n + 2)
                ve.reciprocal(row_inv[:, 2 * n:2 * n + 2], row_sum[:, 2 * n:2 * n + 2]).then_inc(inv_done, 1)

            def store_probT(n):
                dve.wait_ge(probT_psum, 2 * n + 1)
                if n >= 1:
                    dve.wait_ge(attn_psum, n)
                ve.tensor_copy(probT[:, 0, 0:keys(n)], bank[4][:, 0:keys(n)]).then_inc(probT_done[0], 1)

            def add_mix(i, half):
                dve.wait_ge(mix_psum, 2 * i + half + 1)
                part = resid[:, i, half * 512:(half + 1) * 512]
                ve.tensor_tensor(part, part, bank[7][:, :], ALU.add).then_inc(mix_done, 1)

            def keep_logits(i):
                dve.wait_ge(logit_psum, i + 1)
                ve.tensor_copy(logits[:, i, :], bank[7][:, 0:GROUPS + EXPERTS]).then_inc(logit_done, 1)

            LAG = 3
            for n in range(UNITS + LAG):
                if n < UNITS:
                    mask(n)
                if 1 <= n <= UNITS:
                    invert(n - 1)
                if 2 <= n < UNITS + 2:
                    store_probT(n - 2)
                i, step = divmod(n - LAG - PAIRS, PAIRS)
                if i >= 0 and step < 2:
                    add_mix(i, step)
                if i >= 0 and step == 4:
                    keep_logits(i)
            add_mix(TILES - 1, 0)
            add_mix(TILES - 1, 1)
            dve.wait_ge(std2_done, 1)
            ve.reciprocal(rstd2, std2).then_inc(rstd2_ready, 1)
            keep_logits(TILES - 1)

            steps = [0]

            def then(instruction):
                steps[0] += 1
                instruction.then_inc(rt_dve, 1)
                dve.wait_ge(rt_dve, steps[0])

            def wide(a, n):
                return a[:, :, None].to_broadcast([P, TILES, n])

            def same(name, n):
                return const(name)[:, None, :].to_broadcast([P, TILES, n])

            n_log = GROUPS + EXPERTS
            dve.wait_ge(logit_done, TILES)
            dve.wait_ge(rstd2_ready, 1)
            then(ve.tensor_tensor(scaled, logits, wide(rstd2, n_log), ALU.mult))
            then(ve.tensor_tensor(scaled, scaled, same("bias", n_log), ALU.add))
            glog = scaled[:, :, 0:GROUPS]
            elog = scaled[:, :, GROUPS:n_log]
            then(ve.tensor_reduce(group_top, glog, AX.X, ALU.max))
            ve.tensor_tensor(group_low, glog, wide(group_top, GROUPS), ALU.subtract).then_inc(low_ready, 1)
            then(ve.tensor_tensor(group_is, glog, wide(group_top, GROUPS), ALU.is_equal))
            then(ve.tensor_tensor(group_val, group_is, same("first8", GROUPS), ALU.mult))
            then(ve.tensor_reduce(group_first, group_val, AX.X, ALU.max))
            then(ve.tensor_tensor(group_is, group_val, wide(group_first, GROUPS), ALU.is_equal))
            then(ve.tensor_scalar(group_val, group_is, -NEVER, NEVER, ALU.mult, ALU.add))
            then(ve.tensor_tensor(cand.rearrange("p t (g e) -> p t g e", g=GROUPS),
                                  elog.rearrange("p t (g e) -> p t g e", g=GROUPS),
                                  group_val[:, :, :, None].to_broadcast([P, TILES, GROUPS, PER_GROUP]), ALU.add))
            for c in range(2):
                then(ve.tensor_reduce(top[c], cand, AX.X, ALU.max))
                then(ve.tensor_tensor(is_top, cand, wide(top[c], EXPERTS), ALU.is_equal))
                then(ve.tensor_tensor(top_val, is_top, same("first64", EXPERTS), ALU.mult))
                then(ve.tensor_reduce(first[c], top_val, AX.X, ALU.max))
                then(ve.tensor_tensor(chosen[c], top_val, wide(first[c], EXPERTS), ALU.is_equal))
                if c == 0:
                    then(ve.scalar_tensor_tensor(cand, chosen[0], 3 * NEVER, cand, ALU.mult, ALU.add))
            ve.tensor_tensor(gap, top[1], top[0], ALU.subtract).then_inc(gap_ready, 1)
            ve.tensor_tensor(picked, chosen[0], chosen[1], ALU.add).then_inc(picked_ready, 1)
            dve.wait_ge(gexp_done, 1)
            then(ve.tensor_reduce(group_sum, group_exp, AX.X, ALU.add))
            then(ve.reciprocal(group_prob, group_sum))
            dve.wait_ge(ratio_done, 1)
            then(ve.tensor_scalar(denom, ratio, 1.0, None, ALU.add))
            then(ve.reciprocal(inv, denom))
            then(ve.tensor_tensor(gate[0], inv, group_prob, ALU.mult))
            then(ve.tensor_tensor(gate[1], gate[0], ratio, ALU.mult))
            then(ve.tensor_tensor(gated, chosen[0], wide(gate[0], EXPERTS), ALU.mult))
            then(ve.tensor_tensor(weight[:, :, 0:EXPERTS], chosen[1], wide(gate[1], EXPERTS), ALU.mult))
            then(ve.tensor_tensor(weight[:, :, 0:EXPERTS], weight[:, :, 0:EXPERTS], gated, ALU.add))
            then(ve.tensor_copy(weight[:, :, EXPERTS:EXPERTS + AHEAD], weight[:, :, 0:AHEAD]))
            dve.wait_ge(rank_psum, 1)
            then(ve.scalar_tensor_tensor(ranked, bank[0][:, 0:TILES * EXPERTS].rearrange("p (t e) -> p t e", t=TILES),
                                         1.0, picked, ALU.add, ALU.mult))
            then(ve.tensor_scalar(rank[:, :, 0:EXPERTS], ranked, -1.0, None, ALU.add))
            then(ve.tensor_scalar(rank[:, :, EXPERTS:EXPERTS + AHEAD], rank[:, :, 0:AHEAD], -float(SLOTS), None,
                                  ALU.add))
            then(ve.tensor_reduce(fullest, bank[1][:, 0:EXPERTS], AX.X, ALU.max))
            then(ve.tensor_scalar(is_round, const("round_start"), fullest, None, ALU.is_lt))
            then(ve.tensor_reduce(rounds_f, is_round, AX.X, ALU.add))
            then(ve.tensor_copy(counts_i[:, 1:2], rounds_f))
            then(ve.tensor_scalar(counts_i[:, 0:1], rounds_f, float(ITERS), None, ALU.mult))
            ve.tensor_copy(slot_now, const("slot")).then_inc(routing_done, 1)
            dve.wait_ge(routing_done, 1)

            for t in range(TILES):
                ve.tensor_scalar(h2[:, t], resid[:, t, :].rearrange("p (d k) -> p k d", k=CHUNKS),
                                 rstd2[:, t:t + 1], None, ALU.mult).then_inc(h2_done, 1)
            ve.memset(y_rows[:, 1, :], 0.0).then_inc(y_done_dve, 1)
            ve.memset(spread[:, 1], 0.0).then_inc(spread_done, 1)
            dve.sem_inc(added, 1)

            def store_xT(part, b):
                ps = bank[part % 2][:, 0:2 * P]
                ve.tensor_tensor(xT[:, b, 2 * part:2 * part + 2, :], ps.rearrange("p (c s) -> p c s", c=2),
                                 const("gain_ffn_gather")[:, 2 * part:2 * part + 2, None].to_broadcast([P, 2, P]),
                                 ALU.mult).then_inc(xT_done, 1)

            def add_back(t, half):
                part = resid[:, t, half * 512:(half + 1) * 512]
                return ve.tensor_tensor(part, part, bank[7][:, :], ALU.add)

            def pick_set(b, column):
                ve.tensor_tensor(pick[:, b].rearrange("p t (e s) -> p t e s", e=SET),
                                 slot_now[:, None, None, :].to_broadcast([P, TILES, SET, SLOTS]),
                                 rank[:, :, bass.ds(column, SET)][:, :, :, None].to_broadcast([P, TILES, SET, SLOTS]),
                                 ALU.is_equal).then_inc(pick_done, 1)

            for b in range(2):
                pick_set(b, b * SET)
            for part in range(4):
                dve.wait_ge(gather_psum, part + 1)
                store_xT(part, 0)
            rounds = dve.value_load(counts_i[0:1, 1:2], min_val=1, max_val=MAX_ROUNDS)

            def vector_pass(r, it):
                for u in range(ITER):
                    b, e = divmod(u, SET)
                    done = r * EXPERTS + (it * ITER + u)
                    sets = r * (2 * ITERS) + (it * 2 + b)
                    dve.wait_ge(silu_done, done + 1)
                    ve.tensor_tensor(hidden, hidden_gate, bank[2 + u % 2][:, P:2 * P], ALU.mult
                                     ).then_inc(hidden_done, 1)
                    for half in range(2):
                        dve.wait_ge(combine_psum, done * 2 + half + 1)
                        add_back(e, half).then_inc(added, 1)
                    dve.wait_ge(gather_psum, done + SET + 1)
                    store_xT(e, 1 - b)
                    dve.wait_ge(down_psum, done + 1)
                    for q in range(2, 4):
                        last = ve.tensor_copy(y_rows[SLOTS * e:SLOTS * (e + 1), b, q * 256:(q + 1) * 256],
                                              bank[6][SLOTS * q:SLOTS * (q + 1), 0:256])
                    last.then_inc(y_done_dve, 1)
                    if e == 1:
                        dve.wait_ge(gather_psum, sets * SET + SET)
                        dve.wait_ge(pickg_done, sets + 1)
                        pick_set(b, it * (2 * SET) + (AHEAD + b * SET))

            with dve.Fori(0, rounds) as r:
                with dve.Fori(0, ITERS) as it:
                    vector_pass(r, it)
                dve.wait_ge(pick_done, r * (2 * ITERS) + (2 * ITERS + 2))
                ve.tensor_scalar(slot_now, slot_now, float(SLOTS), None, ALU.add).then_inc(slot_ready, 1)
                dve.wait_ge(slot_ready, r + 1)
            for t in range(TILES):
                for half in range(2):
                    dve.wait_ge(combine_psum, rounds * (2 * EXPERTS) + (2 * t + half + 1))
                    add_back(t, half).then_inc(added, 1)

        @block.gpsimd
        def _(pool):
            gp = nc.gpsimd
            gp.memset(ones_bf[:, :], 1.0).then_inc(pool_step, 1)
            pool.wait_ge(pool_step, 1)
            gp.memset(kTz[DH:P, 0], 0.0).then_inc(pool_step, 1)
            pool.wait_ge(pool_step, 2)
            gp.memset(kTz[0:DH, 1], 0.0).then_inc(pool_step, 1)
            pool.wait_ge(pool_step, 3)
            pool.wait_ge(params_in, 16)
            gp.tensor_copy(earlier_bf[:, :], const("earlier")).then_inc(pool_step, 1)
            pool.wait_ge(pool_step, 4)
            gp.tensor_tensor(router, router,
                             const("gain_ffn_router")[:, :, None].to_broadcast([P, CHUNKS, P]), ALU.mult
                             ).then_inc(tables_ready, 1)
            for n in range(UNITS):
                pool.wait_ge(inv_done, n + 1)
                for z in range(2):
                    h, w = 2 * n + z, keys(n)
                    gp.tensor_scalar(prob[:, h % N_PROB, 0:w], prob[:, h % N_PROB, 0:w], row_inv[:, h:h + 1], None,
                                     ALU.mult).then_inc(prob_done, 1)

            def gate_set(b, column):
                gp.tensor_tensor(pick_gated[:, b].rearrange("p t (e s) -> p t e s", e=SET),
                                 pick[:, b].rearrange("p t (e s) -> p t e s", e=SET),
                                 weight[:, :, bass.ds(column, SET)][:, :, :, None].to_broadcast(
                                     [P, TILES, SET, SLOTS]),
                                 ALU.mult).then_inc(pickg_done, 1)

            pool.wait_ge(routing_done, 1)
            rounds = pool.value_load(counts_i[0:1, 1:2], min_val=1, max_val=MAX_ROUNDS)
            for b in range(2):
                pool.wait_ge(pick_done, b + 1)
                gate_set(b, b * SET)
            with pool.Fori(0, rounds) as r:
                with pool.Fori(0, ITERS) as it:
                    for b in range(2):
                        sets = r * (2 * ITERS) + it * 2 + b
                        pool.wait_ge(pick_done, sets + 3)
                        pool.wait_ge(spread_psum, sets + 1)
                        gate_set(b, it * (2 * SET) + (AHEAD + b * SET))


def kernel(**inputs):
    import concourse.bacc as bacc
    from concourse.bass_utils import run_bass_kernel_spmd

    a = {k: np.asarray(v) for k, v in inputs.items()}
    parts = constants()
    per_chunk = lambda g: g.reshape(CHUNKS, P).T
    parts["gain_mix"] = per_chunk(a["norm_mix"][0])
    parts["gain_ffn_router"] = per_chunk(a["norm_ffn"][0])
    parts["gain_ffn_gather"] = a["norm_ffn"][0].reshape(P, CHUNKS)
    parts["q_gain"] = np.tile(a["attn_q_norm"][0], 2)[:, None]
    parts["k_gain"] = np.tile(a["attn_k_norm"][0], 2)[:, None]
    parts["bias"] = np.tile(np.concatenate([a["moe_b_group"][0], a["moe_b_expert"][0]]), (P, 1))
    router = np.zeros((D, P), np.float32)
    router[:, 0:GROUPS] = a["moe_w_group"][0]
    router[:, GROUPS:GROUPS + EXPERTS] = a["moe_w_expert"][0]
    parts["router"] = router.reshape(CHUNKS, P, P).transpose(1, 0, 2).reshape(P, CHUNKS * P)
    params = np.empty((P, PARAMS), np.float32)
    for name, (lo, hi) in COLS.items():
        params[:, lo:hi] = parts[name]

    arrays = dict(x=a["x"][0], params=params, w_in=a["attn_w_in"][0], w_out=a["attn_w_out"][0],
                  w_gate=a["moe_w_gate"][0], w_up=a["moe_w_up"][0], w_down=a["moe_w_down"][0])
    arrays = {k: np.ascontiguousarray(v) for k, v in arrays.items()}
    nc = bacc.Bacc("TRN2", target_bir_lowering=False, num_devices=1)
    args = {k: nc.dram_tensor(k, v.shape, mybir.dt.from_np(v.dtype), kind="ExternalInput").ap()
            for k, v in arrays.items()}
    out = nc.dram_tensor("out", (SEQ, D), F32, kind="ExternalOutput").ap()
    trunk(nc, out=out, **args)
    result = run_bass_kernel_spmd(nc, [arrays], core_ids=[0])
    return result.results[0]["out"].reshape(1, SEQ, D)
```

```python
from contextlib import ExitStack

import numpy as np

import concourse.bass as bass
from concourse import mybir

F32 = mybir.dt.float32
F32R = mybir.dt.float32r
BF16 = mybir.dt.bfloat16
I32 = mybir.dt.int32
ACT = mybir.ActivationFunctionType
ALU = mybir.AluOpType
AX = mybir.AxisListType

P = 128
SEQ, D = 512, 1024
TILES = SEQ // P
CHUNKS = D // P
HEADS, DH = 16, 64
PAIRS = HEADS // 2
BRANCHES = ((128, 1), (512, 4), (2048, 16))
EPS = 1e-6
GROUPS, PER_GROUP = 8, 8
EXPERTS = GROUPS * PER_GROUP
FF = D // 2
FQ = FF // P
SLOTS = 32
SET = P // SLOTS
MAX_ROUNDS = SEQ // SLOTS
NEVER = -1.0e30
PIECE = 4096
RING = 8
LOADS = 3 * RING

_WIDTHS = dict(ident=P, logmult=SEQ, gain_mix=CHUNKS, gain_ffn_gather=CHUNKS, gain_ffn_router=CHUNKS, q_gain=1,
               k_gain=1, eps=1, bias=GROUPS + EXPERTS, first8=GROUPS, first64=EXPERTS, slot=SLOTS,
               round_start=MAX_ROUNDS, earlier=P, router=CHUNKS * P)
COLS, _at = {}, 0
for _name, _w in _WIDTHS.items():
    COLS[_name] = (_at, _at + _w)
    _at += _w
PARAMS = _at
EARLY = COLS["router"][0]


def matrix_of(n):
    e, j = divmod(n, 3)
    crosses = 3 * e % RING == RING - 1
    return e, (j - 1) % 3 if crosses else j


LOAD_OF = {matrix_of(n): n for n in range(LOADS)}


def constants():
    d = (SEQ - P) + np.arange(P)[:, None] - np.arange(SEQ)[None, :]
    times = sum(((d >= 0) & (d % dil == 0) & (d <= win)).astype(np.float64) for win, dil in BRANCHES)
    return dict(
        ident=np.eye(P),
        logmult=np.where(times > 0, np.log(np.maximum(times, 1)), NEVER),
        eps=np.full((P, 1), EPS),
        first8=np.tile(GROUPS - np.arange(GROUPS), (P, 1)),
        first64=np.tile(EXPERTS - np.arange(EXPERTS), (P, 1)),
        slot=np.tile(np.arange(SLOTS), (P, 1)),
        round_start=np.tile(SLOTS * np.arange(MAX_ROUNDS), (P, 1)),
        earlier=np.triu(np.ones((P, P)), 1),
    )


def trunk(nc, x, params, w_in, w_out, w_gate, w_up, w_down, out):
    ctx = ExitStack()
    with ctx:
        def sem(name):
            return ctx.enter_context(nc.semaphore(name))

        REGION = 4096
        PAR = -(-PARAMS // 8) * 8
        SMALL = PAR + 3 * 512 + 290
        ring_sb = ctx.enter_context(nc.sbuf_tensor("ring", [P, RING * PIECE], F32))
        regions = ctx.enter_context(nc.sbuf_tensor("regions", [P, 4 * REGION], F32))
        smalls = ctx.enter_context(nc.sbuf_tensor("smalls", [P, SMALL], F32))
        taken = [0]

        def take(n):
            taken[0] += n
            assert taken[0] <= SMALL
            return smalls[:, taken[0] - n:taken[0]]

        ring = ring_sb[:, :].rearrange("p (s n) -> p s n", s=RING)
        region_q = ring[:, RING - 2, :]
        region_v = ring[:, RING - 1, :]
        resid = regions[:, 0:REGION].rearrange("p (t n) -> p t n", t=TILES)
        region_h = regions[:, REGION:2 * REGION]
        region_k = regions[:, 2 * REGION:4 * REGION]
        par_sb = take(PAR)
        chunk_at = taken[0]
        qk_norm = take(2 * 512).rearrange("p (b n) -> p b n", b=2)
        squares = take(512)

        def const(name):
            a, b = COLS[name]
            return par_sb[:, a:b]

        ident = const("ident")
        router = const("router").rearrange("p (c n) -> p c n", c=CHUNKS)

        def over(name, memory, at, *shape):
            return nc.alloc_sbuf_tensor_at(name, [P, *shape], F32R, offset=nc.lookup_mloc(memory).addr + 4 * at)

        hT_hi = over("hT_hi", regions, REGION, CHUNKS, SEQ)
        hT_lo = over("hT_lo", ring_sb, 1 * PIECE, CHUNKS, SEQ)
        raw = ring[:, 0, :].rearrange("p (f n) -> p f n", f=2)
        w_hi = over("w_hi", ring_sb, 2 * PIECE, 2, CHUNKS, 512)
        w_lo = over("w_lo", ring_sb, 4 * PIECE, 2, CHUNKS, 512)
        raw_out = ring[:, 0:2, :]
        w_out_hi = w_hi[:, :, :, :].rearrange("p b c n -> p (b c n)").rearrange("p (c n) -> p c n", c=CHUNKS)
        w_out_lo = w_lo[:, :, :, :].rearrange("p b c n -> p (b c n)").rearrange("p (c n) -> p c n", c=CHUNKS)
        oT_hi = over("oT_hi", ring_sb, (RING - 2) * PIECE, PAIRS, SEQ)
        OT_LO = 9
        oT_lo = over("oT_lo", smalls, chunk_at, OT_LO, P)
        qT = region_q.rearrange("p (m s) -> p m s", m=PAIRS)
        kTz = region_k.rearrange("p (z m s) -> p z m s", z=2, m=PAIRS)
        v = region_v.rearrange("p (t n) -> p t n", t=TILES)
        N_PROB = 6
        prob = region_h[:, 0:N_PROB * 512].rearrange("p (b n) -> p b n", b=N_PROB)
        probT = region_h[:, N_PROB * 512:REGION].rearrange("p (b n) -> p b n", b=2)

        h2 = region_h.rearrange("p (t k d) -> p t k d", t=TILES, k=CHUNKS)
        xT = region_k.rearrange("p (b k s) -> p b k s", b=8, k=CHUNKS)[:, 0:2]
        y_rows = region_k.rearrange("p (b n) -> p b n", b=8)[:, 2:4, :]
        pick = region_k.rearrange("p (b t s) -> p b t s", b=16, t=TILES)[:, 8:10]
        pick_gated = region_k.rearrange("p (b t s) -> p b t s", b=16, t=TILES)[:, 10:12]
        spread = region_k.rearrange("p (b t s) -> p b t s", b=16, t=TILES)[:, 12:14]
        hidden_gate = region_k[:, 14 * 512:14 * 512 + P]
        hidden = region_k[:, 14 * 512 + P:14 * 512 + 2 * P]
        hiddenT = region_k[:, 14 * 512 + 2 * P:14 * 512 + 3 * P]

        rt = [0]

        def rview(*shape):
            n = int(np.prod(shape))
            a = region_k[:, rt[0]:rt[0] + n]
            rt[0] += n
            assert rt[0] <= 3 * 1024
            if len(shape) == 2:
                a = a.rearrange("p (a b) -> p a b", a=shape[0])
            return a

        log_at = OT_LO * P
        logits = smalls[:, chunk_at + log_at:chunk_at + log_at + TILES * (GROUPS + EXPERTS)].rearrange(
            "p (t n) -> p t n", t=TILES)
        scaled = rview(TILES, GROUPS + EXPERTS)
        group_top = rview(TILES)
        group_low = rview(TILES, GROUPS)
        group_exp = rview(TILES, GROUPS)
        group_sum = rview(TILES)
        group_prob = rview(TILES)
        group_is = rview(TILES, GROUPS)
        group_val = rview(TILES, GROUPS)
        group_first = rview(TILES)
        cand = rview(TILES, EXPERTS)
        is_top = rview(TILES, EXPERTS)
        top_val = rview(TILES, EXPERTS)
        top = [rview(TILES), rview(TILES)]
        first = [rview(TILES), rview(TILES)]
        chosen = [rview(TILES, EXPERTS), rview(TILES, EXPERTS)]
        gap = rview(TILES)
        ratio = rview(TILES)
        denom = rview(TILES)
        inv = rview(TILES)
        gate = [rview(TILES), rview(TILES)]
        gated = rview(TILES, EXPERTS)
        AHEAD = 2 * SET
        kept = 14 * 512 + 3 * P
        rank = region_k[:, kept:kept + TILES * (EXPERTS + AHEAD)].rearrange("p (t e) -> p t e", t=TILES)
        kept += TILES * (EXPERTS + AHEAD)
        weight = region_k[:, kept:kept + TILES * (EXPERTS + AHEAD)].rearrange("p (t e) -> p t e", t=TILES)
        kept += TILES * (EXPERTS + AHEAD)
        slot_now = region_k[:, kept:kept + SLOTS]
        picked = rview(TILES * EXPERTS // 2).bitcast(BF16).rearrange("p (t e) -> p t e", t=TILES)
        ranked = rview(TILES, EXPERTS)
        fullest = rview(1)
        is_round = rview(MAX_ROUNDS)
        rounds_f = rview(1)
        counts_i = ctx.enter_context(nc.sbuf_tensor("counts_i", [P, 2], I32))
        earlier_bf = ctx.enter_context(nc.sbuf_tensor("earlier_bf", [P, P], BF16))
        ones_bf = ctx.enter_context(nc.sbuf_tensor("ones_bf", [P, P], BF16))

        def small(n):
            return take(n)

        ssq = small(TILES)
        std = small(TILES)
        rstd = small(TILES)
        ssq2 = small(TILES)
        std2 = small(TILES)
        rstd2 = small(TILES)
        head_ssq = small(16).rearrange("p (b n) -> p b n", b=2)
        head_std = small(16).rearrange("p (b n) -> p b n", b=2)
        token_rstd = small(16).rearrange("p (b n) -> p b n", b=2)
        head_rstd = small(16).rearrange("p (b n) -> p b n", b=2)
        qk_scale = small(1)
        neg_max = small(TILES * HEADS)
        row_sum = small(TILES * HEADS)
        row_inv = small(TILES * HEADS)

        bank = [ctx.enter_context(nc.psum_tensor(f"bank{i}", [P, 512], F32)) for i in range(8)]

        x_in = [sem(f"x_in{t}") for t in range(TILES)]
        params_in = sem("params_in")
        router_in = sem("router_in")
        raw_in = [sem("raw_in0"), sem("raw_in1")]
        hi_done = sem("hi_done")
        split_done = sem("split_done")
        ring_in = [sem(f"ring_in{s}") for s in range(RING)]
        tables_ready = sem("tables_ready")
        pool_step = sem("pool_step")
        qk_scale_ready = sem("qk_scale_ready")
        ssq_done = sem("ssq_done")
        std_done = sem("std_done")
        rstd_done = sem("rstd_done")
        xT_psum = sem("xT_psum")
        hT_hi_done = sem("hT_hi_done")
        hT_done = sem("hT_done")
        proj_done = sem("proj_done")
        sq_done = sem("sq_done")
        hssq_done = sem("hssq_done")
        hstd_done = sem("hstd_done")
        hrstd_done = sem("hrstd_done")
        trstd_done = sem("trstd_done")
        qk_normed = sem("qk_normed")
        qkT_psum = sem("qkT_psum")
        qkT_done = sem("qkT_done")
        v_done = sem("v_done")
        score_done = sem("score_done")
        masked_done = sem("masked_done")
        exp_done = sem("exp_done")
        inv_done = sem("inv_done")
        prob_done = sem("prob_done")
        probT_psum = sem("probT_psum")
        probT_done = [sem("probT_done_even"), sem("probT_done_odd")]
        attn_psum = sem("attn_psum")
        attn_hi_done = sem("attn_hi_done")
        attn_done = sem("attn_done")
        mix_psum = sem("mix_psum")
        mix_done = sem("mix_done")
        ssq2_done = sem("ssq2_done")
        x2T_psum = sem("x2T_psum")
        x2T_done = sem("x2T_done")
        logit_psum = sem("logit_psum")
        logit_done = sem("logit_done")
        rt_dve = sem("rt_dve")
        std2_done = sem("std2_done")
        rstd2_ready = sem("rstd2_ready")
        low_ready = sem("low_ready")
        gexp_done = sem("gexp_done")
        gap_ready = sem("gap_ready")
        ratio_done = sem("ratio_done")
        picked_ready = sem("picked_ready")
        rank_psum = sem("rank_psum")
        routing_done = sem("routing_done")
        h2_done = sem("h2_done")
        slot_ready = sem("slot_ready")
        pick_done = sem("pick_done")
        pickg_done = sem("pickg_done")
        gather_psum = sem("gather_psum")
        xT_done = sem("xT_done")
        up_psum = sem("up_psum")
        silu_done = sem("silu_done")
        hidden_done = sem("hidden_done")
        hiddenT_psum = sem("hiddenT_psum")
        hiddenT_done = sem("hiddenT_done")
        spread_psum = sem("spread_psum")
        spread_done = sem("spread_done")
        down_psum = sem("down_psum")
        y_done_act = sem("y_done_act")
        y_done_dve = sem("y_done_dve")
        combine_psum = sem("combine_psum")
        added = sem("added")
        out_stored = sem("out_stored")

        BLOCKS = 6
        QK_UNITS = 4 * TILES
        UNITS = TILES * PAIRS
        ITER = 2 * SET
        ITERS = EXPERTS // ITER

        def x2T_bank(i, half):
            return 6 if i == TILES - 1 and half == 1 else 7

        def keys(n):
            return (n // PAIRS + 1) * P

        gate_v = w_gate.rearrange("e (p k) n -> e p (k n)", k=CHUNKS)
        up_v = w_up.rearrange("e (p k) n -> e p (k n)", k=CHUNKS)
        down_v = w_down.rearrange("e (j p) n -> e p j n", p=P)
        HALVES = 2 * BLOCKS

        block = ctx.enter_context(nc.Block())

        @block.sync
        def _(sp):
            def load_x(t):
                sp.dma_start(resid[:, t, :], x[t * P:(t + 1) * P, :]).then_inc(x_in[t], 16)

            def load_w_in(f):
                b, half = divmod(f, 2)
                if f >= 2:
                    sp.wait_ge(split_done, f - 1)
                sp.dma_start(raw[:, half, :].rearrange("p (c n) -> p c n", c=4),
                             w_in[half * 512:(half + 1) * 512, b * 512:(b + 1) * 512].rearrange(
                                 "(c p) n -> p c n", p=P)).then_inc(raw_in[half], 16)

            load_x(0)
            sp.dma_start(par_sb[:, 0:EARLY], params[:, 0:EARLY]).then_inc(params_in, 16)
            load_w_in(0)
            load_x(1)
            load_w_in(1)
            load_x(2)
            load_x(3)
            sp.dma_start(par_sb[:, EARLY:PARAMS], params[:, EARLY:PARAMS]).then_inc(router_in, 16)
            for f in range(2, HALVES):
                load_w_in(f)
            for half in range(2):
                if half == 0:
                    sp.wait_ge(split_done, HALVES)
                else:
                    sp.wait_ge(proj_done, BLOCKS * TILES)
                sp.dma_start(raw_out[:, half, :].rearrange("p (c n) -> p c n", c=4),
                             w_out[half * 512:(half + 1) * 512, :].rearrange("(c p) n -> p c n", p=P)
                             ).then_inc(raw_in[half], 16)

            def load(n, first_expert):
                e, what = matrix_of(n)
                piece, expert = ring[:, n % RING, :], first_expert + e
                if what == 2:
                    sp.dma_start(piece.rearrange("p (j n) -> p j n", j=FQ), down_v[expert]
                                 ).then_inc(ring_in[n % RING], 16)
                else:
                    sp.dma_start(piece, (gate_v, up_v)[what][expert]).then_inc(ring_in[n % RING], 16)

            def wait_used(n, experts_before):
                e, what = matrix_of((n - RING) % LOADS)
                if n < RING:
                    e -= RING
                sp.wait_ge(down_psum if what == 2 else up_psum, experts_before + (e + 1))

            for n in range(LOADS):
                if n == 0:
                    sp.wait_ge(split_done, HALVES + 2)
                elif n == 1:
                    sp.wait_ge(split_done, HALVES + 4)
                elif n == 2:
                    sp.wait_ge(mix_psum, 2 * TILES)
                elif n == RING - 2:
                    sp.wait_ge(logit_psum, TILES)
                    sp.wait_ge(ssq2_done, TILES)
                elif n == RING - 1:
                    sp.wait_ge(attn_psum, UNITS)
                elif n >= RING:
                    wait_used(n, 0)
                load(n, 0)
            with sp.Fori(1, EXPERTS // RING) as turn:
                for n in range(LOADS):
                    wait_used(n, turn * RING)
                    load(n, turn * RING)
            sp.wait_ge(routing_done, 1)
            rounds = sp.value_load(counts_i[0:1, 1:2], min_val=1, max_val=MAX_ROUNDS)
            with sp.If(rounds > 1):
                with sp.Fori(1, rounds) as r:
                    with sp.Fori(0, EXPERTS // RING) as turn:
                        for n in range(LOADS):
                            wait_used(n, r * EXPERTS + turn * RING)
                            load(n, turn * RING)
            for t in range(TILES):
                sp.wait_ge(added, rounds * (2 * EXPERTS) + (2 * t + 3))
                sp.dma_start(out[t * P:(t + 1) * P, :], resid[:, t, :]).then_inc(out_stored, 16)
            sp.wait_ge(out_stored, 16 * TILES)

        @block.tensor
        def _(pe):
            mm, tr = nc.tensor.matmul, nc.tensor.transpose
            pe.wait_ge(params_in, 16)

            for t in range(TILES):
                pe.wait_ge(x_in[t], 16)
                for half in range(2):
                    b = 4 + (2 * t + half) % 4
                    if t >= 2:
                        pe.wait_ge(hT_done, 2 * (t - 2) + half + 1)
                    for c in range(4):
                        last = tr(bank[b][:, c * P:(c + 1) * P],
                                  resid[:, t, (4 * half + c) * P:(4 * half + c + 1) * P], ident)
                    last.then_inc(xT_psum, 1)

            def split_product(out, hi, lo, w_hi_c, w_lo_c, first, final):
                mm(out, hi, w_hi_c, start=first, stop=False)
                mm(out, hi, w_lo_c, start=False, stop=False)
                return mm(out, lo, w_hi_c, start=False, stop=final)

            def project(u):
                b, t = divmod(u, TILES)
                if u < TILES:
                    pe.wait_ge(hT_done, 2 * (t + 1))
                if u >= 2:
                    if u - 2 < QK_UNITS:
                        pe.wait_ge(qk_normed, u - 1)
                    else:
                        pe.wait_ge(v_done, u - 1 - QK_UNITS)
                for c in range(CHUNKS):
                    if t == 0 and c % 4 == 0:
                        pe.wait_ge(split_done, 2 * b + c // 4 + 1)
                    last = split_product(bank[u % 2][:, :], hT_hi[:, c, t * P:(t + 1) * P],
                                         hT_lo[:, c, t * P:(t + 1) * P], w_hi[:, b % 2, c, :], w_lo[:, b % 2, c, :],
                                         c == 0, c == CHUNKS - 1)
                last.then_inc(proj_done, 1)

            def turn_qk(u):
                pe.wait_ge(qk_normed, u + 1)
                if u >= 2:
                    pe.wait_ge(qkT_done, u - 1)
                for c in range(4):
                    last = tr(bank[2 + u % 2][:, c * P:(c + 1) * P], qk_norm[:, u % 2, c * P:(c + 1) * P], ident)
                last.then_inc(qkT_psum, 1)

            for u in range(BLOCKS * TILES):
                project(u)
                if 1 <= u <= QK_UNITS:
                    turn_qk(u - 1)

            def scores(n):
                i, m = divmod(n, PAIRS)
                if n == 0:
                    pe.wait_ge(qkT_done, QK_UNITS)
                    pe.wait_ge(v_done, 2 * TILES)
                for z in range(2):
                    if n >= 2:
                        pe.wait_ge(masked_done, 2 * (n - 2) + z + 1)
                    mm(bank[2 * (n % 2) + z][:, 0:keys(n)], qT[:, m, i * P:(i + 1) * P], kTz[:, z, m, 0:keys(n)],
                       start=True, stop=True).then_inc(score_done, 1)

            def turn_probs(n):
                for z in range(2):
                    pe.wait_ge(prob_done, 2 * n + z + 1)
                    if n >= 1:
                        pe.wait_ge(probT_done[z], n)
                    for kb in range(n // PAIRS + 1):
                        last = tr(bank[4 + z][:, kb * P:(kb + 1) * P],
                                  prob[:, (2 * n + z) % N_PROB, kb * P:(kb + 1) * P], ident)
                    last.then_inc(probT_psum, 1)

            def attend(n):
                i, m = divmod(n, PAIRS)
                pe.wait_ge(probT_done[0], n + 1)
                pe.wait_ge(probT_done[1], n + 1)
                if n >= 1:
                    pe.wait_ge(attn_done, n)
                for kb in range(i + 1):
                    for z in range(2):
                        last = mm(bank[6][z * DH:(z + 1) * DH, 0:P],
                                  v[:, kb, (2 * m + z) * DH:(2 * m + z + 1) * DH],
                                  probT[:, z, kb * P:(kb + 1) * P],
                                  start=(kb == 0), stop=(kb == i))
                last.then_inc(attn_psum, 1)

            def mix(i, half):
                if half == 0:
                    pe.wait_ge(attn_done, PAIRS * (i + 1))
                if i == 0 and half == 0:
                    pe.wait_ge(split_done, HALVES + 4)
                if half == 1:
                    pe.wait_ge(mix_done, 2 * i + 1)
                elif i >= 1:
                    pe.wait_ge(logit_done, i)
                for c in range(CHUNKS):
                    cols = slice(half * 512, (half + 1) * 512)
                    last = split_product(bank[7][:, :], oT_hi[:, c, i * P:(i + 1) * P],
                                         oT_lo[:, (PAIRS * i + c) % OT_LO, :], w_out_hi[:, c, cols],
                                         w_out_lo[:, c, cols], c == 0, c == CHUNKS - 1)
                last.then_inc(mix_psum, 1)

            def turn_x2(i, half):
                pe.wait_ge(mix_done, 2 * (i + 1))
                if half == 1 and i < TILES - 1:
                    pe.wait_ge(x2T_done, 2 * i + 1)
                for c in range(4):
                    last = tr(bank[x2T_bank(i, half)][:, c * P:(c + 1) * P],
                              resid[:, i, (4 * half + c) * P:(4 * half + c + 1) * P], ident)
                last.then_inc(x2T_psum, 1)

            def route(i):
                pe.wait_ge(x2T_done, 2 * (i + 1))
                pe.wait_ge(tables_ready, 1)
                for c in range(CHUNKS):
                    last = mm(bank[7][:, 0:P], qT[:, c, i * P:(i + 1) * P], router[:, c, :],
                              start=(c == 0), stop=(c == CHUNKS - 1))
                last.then_inc(logit_psum, 1)

            def tail(i, step):
                if step == 0:
                    mix(i, 0)
                    mix(i, 1)
                elif step <= 2:
                    turn_x2(i, step - 1)
                else:
                    route(i)

            LAG = 3
            for n in range(UNITS + LAG):
                if n < UNITS:
                    scores(n)
                if n >= LAG:
                    attend(n - LAG)
                if 2 <= n < UNITS + 2:
                    turn_probs(n - 2)
                i, step = divmod(n - LAG - PAIRS, PAIRS)
                if i >= 0 and step < 4:
                    tail(i, step)
            for step in range(4):
                tail(TILES - 1, step)

            pe.wait_ge(picked_ready, 1)
            pe.wait_ge(tables_ready, 1)
            for t in range(TILES):
                for s in range(t + 1):
                    mm(bank[0][:, t * EXPERTS:(t + 1) * EXPERTS], earlier_bf[:, :] if s == t else ones_bf[:, :],
                       picked[:, s, :], start=(s == 0), stop=(s == t))
            for t in range(TILES):
                last = mm(bank[1][:, 0:EXPERTS], ones_bf[:, :], picked[:, t, :], start=(t == 0), stop=(t == TILES - 1))
            last.then_inc(rank_psum, 1)

            def gather(part, picks):
                b = part % 2
                for c in range(2):
                    for t in range(TILES):
                        last = mm(bank[b][:, c * P:(c + 1) * P], h2[:, t, 2 * part + c, :],
                                  picks[:, t, :], start=(t == 0), stop=(t == TILES - 1))
                last.then_inc(gather_psum, 1)

            def combine(t, half, b, to=7):
                return mm(bank[to][:, :], spread[:, b, t, :], y_rows[:, b, half * 512:(half + 1) * 512],
                          start=True, stop=True).then_inc(combine_psum, 1)

            pe.wait_ge(routing_done, 1)
            passes = pe.value_load(counts_i[0:1, 0:1], min_val=ITERS, max_val=ITERS * MAX_ROUNDS)
            pe.wait_ge(h2_done, TILES)
            pe.wait_ge(pick_done, 1)
            for part in range(4):
                if part >= 2:
                    pe.wait_ge(xT_done, part - 1)
                gather(part, pick[:, 0])
            with pe.Fori(0, passes) as it:
                for u in range(ITER):
                    b, e = divmod(u, SET)
                    done = it * ITER + u
                    sets = it * 2 + b
                    n_gate, n_up, n_down = (LOAD_OF[u, what] for what in range(3))
                    s = n_gate % RING
                    if e == 0:
                        pe.wait_ge(xT_done, done + SET)
                    for n in (n_gate, n_up):
                        pe.wait_ge(ring_in[n % RING], it * (16 * LOADS // RING) + 16 * (n // RING + 1))
                    for k in range(CHUNKS):
                        for j in range(FQ):
                            last = mm(bank[2 + u % 2][SLOTS * j:SLOTS * (j + 1), 0:2 * P],
                                      xT[:, b, k, SLOTS * e:SLOTS * (e + 1)],
                                      ring[:, s:s + 2, k * FF + j * P:k * FF + (j + 1) * P],
                                      start=(k == 0), stop=(k == CHUNKS - 1))
                    last.then_inc(up_psum, 1)
                    if e == 0:
                        pe.wait_ge(y_done_act, done + 1)
                        pe.wait_ge(y_done_dve, done + 1)
                        pe.wait_ge(spread_done, sets + 1)
                    for half in range(2):
                        pe.wait_ge(added, done * 2 + (half + 1))
                        combine(e, half, 1 - b)
                    pe.wait_ge(hidden_done, done + 1)
                    tr(bank[4][:, 0:P], hidden, ident).then_inc(hiddenT_psum, 1)
                    if e == 1:
                        pe.wait_ge(pickg_done, sets + 1)
                        for t in range(TILES):
                            last = tr(bank[5][:, t * P:(t + 1) * P], pick_gated[:, b, t, :], ident)
                        last.then_inc(spread_psum, 1)
                    if e == 0:
                        pe.wait_ge(pick_done, sets + 2)
                    pe.wait_ge(xT_done, done + 3)
                    gather(e, pick[:, 1 - b])
                    pe.wait_ge(hiddenT_done, done + 1)
                    pe.wait_ge(ring_in[n_down % RING], it * (16 * LOADS // RING) + 16 * (n_down // RING + 1))
                    pe.wait_ge(y_done_act, done + 1)
                    pe.wait_ge(y_done_dve, done + 1)
                    for j in range(FQ):
                        for q in range(4):
                            last = mm(bank[6][SLOTS * q:SLOTS * (q + 1), 0:256], hiddenT[:, SLOTS * j:SLOTS * (j + 1)],
                                      ring[:, n_down % RING, j * D + q * 256:j * D + (q + 1) * 256],
                                      start=(j == 0), stop=(j == FQ - 1))
                    last.then_inc(down_psum, 1)
            pe.wait_ge(y_done_act, passes * ITER + 1)
            pe.wait_ge(y_done_dve, passes * ITER + 1)
            pe.wait_ge(spread_done, passes * 2 + 1)
            pe.wait_ge(added, passes * (2 * ITER) + 1)
            pe.wait_ge(xT_done, passes * ITER + SET)
            for t in range(TILES):
                for half in range(2):
                    combine(t, half, 1, to=2 * t + half)

        @block.scalar
        def _(act):
            fn = nc.scalar.activation
            act.wait_ge(params_in, 16)
            def split_hi(f):
                if f < HALVES:
                    b, half = divmod(f, 2)
                    act.wait_ge(raw_in[half], 16 * (b + 1))
                    if b >= 2:
                        act.wait_ge(proj_done, TILES * (b - 1))
                    for c in range(4):
                        last = fn(w_hi[:, b % 2, 4 * half + c, :], raw[:, half, c * 512:(c + 1) * 512], ACT.Copy,
                                  scale=const("gain_mix")[:, 4 * half + c:4 * half + c + 1])
                else:
                    half, quarter = divmod(f - HALVES, 2)
                    act.wait_ge(raw_in[half], 16 * (BLOCKS + 1))
                    act.wait_ge(proj_done, TILES * BLOCKS)
                    chunks = slice(4 * half + 2 * quarter, 4 * half + 2 * quarter + 2)
                    last = fn(w_out_hi[:, chunks, :], raw_out[:, half, quarter * 2048:(quarter + 1) * 2048].rearrange(
                        "p (c n) -> p c n", c=2), ACT.Copy)
                last.then_inc(hi_done, 1)

            for t in range(TILES):
                act.wait_ge(x_in[t], 16)
                fn(region_q[:, t * D:(t + 1) * D], resid[:, t, :], ACT.Square,
                   accum_out=ssq[:, t:t + 1]).then_inc(ssq_done, 1)
                for half in range(2):
                    act.wait_ge(xT_psum, 2 * t + half + 1)
                    fn(hT_hi[:, 4 * half:4 * half + 4, t * P:(t + 1) * P],
                       bank[4 + (2 * t + half) % 4][:, :].rearrange("p (c s) -> p c s", c=4), ACT.Copy
                       ).then_inc(hT_hi_done, 1)
                if t < 2:
                    split_hi(t)
            act.wait_ge(ssq_done, TILES)
            fn(std, ssq, ACT.Sqrt, bias=const("eps"), scale=1.0 / D).then_inc(std_done, 1)

            def store_qk(u):
                b, t = divmod(u, TILES)
                act.wait_ge(qkT_psum, u + 1)
                src = bank[2 + u % 2][:, :].rearrange("p (m s) -> p m s", m=4)
                pairs, toks = slice(4 * (b % 2), 4 * (b % 2) + 4), slice(t * P, (t + 1) * P)
                if b < 2:
                    fn(qT[:, pairs, toks], src, ACT.Copy, scale=qk_scale).then_inc(qkT_done, 1)
                else:
                    fn(kTz[0:DH, 0, pairs, toks], src[0:DH], ACT.Copy)
                    fn(kTz[DH:P, 1, pairs, toks], src[DH:P], ACT.Copy).then_inc(qkT_done, 1)

            act.wait_ge(qk_scale_ready, 1)
            act.wait_ge(tables_ready, 1)
            act.wait_ge(rstd_done, 1)
            for u in range(QK_UNITS):
                act.wait_ge(proj_done, u + 1)
                if u >= 1:
                    act.wait_ge(hssq_done, u)
                fn(squares, bank[u % 2][:, :], ACT.Square, scale=rstd[:, u % TILES:u % TILES + 1]
                   ).then_inc(sq_done, 1)
                act.wait_ge(hssq_done, u + 1)
                fn(head_std[:, u % 2, :], head_ssq[:, u % 2, :], ACT.Sqrt, bias=const("eps"),
                   scale=1.0 / DH).then_inc(hstd_done, 1)
                if u >= 1:
                    store_qk(u - 1)
                if u % TILES in (1, 2):
                    split_hi(2 * (u // TILES + 1) + u % TILES - 1)
            for u in range(2 * TILES):
                b, t = divmod(u, TILES)
                act.wait_ge(proj_done, QK_UNITS + u + 1)
                fn(v[:, t, b * 512:(b + 1) * 512], bank[u % 2][:, :], ACT.Copy, scale=rstd[:, t:t + 1]
                   ).then_inc(v_done, 1)
                if u == 0:
                    store_qk(QK_UNITS - 1)
                if b == 0 and t in (1, 2):
                    split_hi(2 * (BLOCKS - 1) + t - 1)

            def exponent(n):
                for z in range(2):
                    h, w = 2 * n + z, keys(n)
                    act.wait_ge(masked_done, h + 1)
                    fn(prob[:, h % N_PROB, 0:w], prob[:, h % N_PROB, 0:w], ACT.Exp, scale=-1.0,
                       bias=neg_max[:, h:h + 1], accum_out=row_sum[:, h:h + 1]).then_inc(exp_done, 1)

            def store_probT(n):
                act.wait_ge(probT_psum, 2 * n + 2)
                if n >= 1:
                    act.wait_ge(attn_psum, n)
                fn(probT[:, 1, 0:keys(n)], bank[5][:, 0:keys(n)], ACT.Copy).then_inc(probT_done[1], 1)

            def store_attn(n):
                i, m = divmod(n, PAIRS)
                act.wait_ge(attn_psum, n + 1)
                fn(oT_hi[:, m, i * P:(i + 1) * P], bank[6][:, 0:P], ACT.Copy).then_inc(attn_hi_done, 1)

            def store_x2T(i, half):
                act.wait_ge(x2T_psum, 2 * i + half + 1)
                fn(qT[:, 4 * half:4 * half + 4, i * P:(i + 1) * P],
                   bank[x2T_bank(i, half)][:, :].rearrange("p (c s) -> p c s", c=4), ACT.Copy).then_inc(x2T_done, 1)

            def square_x2(i):
                act.wait_ge(mix_done, 2 * (i + 1))
                j = max(i - 1, 0)
                act.wait_ge(logit_psum, j + 1)
                fn(qT[:, :, j * P:(j + 1) * P], resid[:, i, :].rearrange("p (c s) -> p c s", c=CHUNKS),
                   ACT.Square, accum_out=ssq2[:, i:i + 1]).then_inc(ssq2_done, 1)

            LAG = 3
            for n in range(UNITS + LAG):
                if n < UNITS:
                    exponent(n)
                if n >= LAG:
                    store_attn(n - LAG)
                if 2 <= n < UNITS + 2:
                    store_probT(n - 2)
                i, step = divmod(n - LAG - PAIRS, PAIRS)
                if n in (3, 4, 5, 6):
                    split_hi(HALVES + n - 3)
                if i >= 0 and step in (1, 2):
                    store_x2T(i, step - 1)
                if i >= 0 and step == 3:
                    square_x2(i)
            square_x2(TILES - 1)
            act.wait_ge(ssq2_done, TILES)
            fn(std2, ssq2, ACT.Sqrt, bias=const("eps"), scale=1.0 / D).then_inc(std2_done, 1)
            store_x2T(TILES - 1, 0)
            store_x2T(TILES - 1, 1)

            act.wait_ge(rstd2_ready, 1)
            for t in range(TILES):
                fn(h2[:, t], resid[:, t, :].rearrange("p (d k) -> p k d", k=CHUNKS), ACT.Copy,
                   scale=rstd2[:, t:t + 1]).then_inc(h2_done, 1)
            act.wait_ge(low_ready, 1)
            fn(group_exp, group_low, ACT.Exp).then_inc(gexp_done, 1)
            act.wait_ge(gap_ready, 1)
            fn(ratio, gap, ACT.Exp).then_inc(ratio_done, 1)

            act.wait_ge(routing_done, 1)
            passes = act.value_load(counts_i[0:1, 0:1], min_val=ITERS, max_val=ITERS * MAX_ROUNDS)
            act.sem_inc(y_done_act, 1)
            with act.Fori(0, passes) as it:
                for u in range(ITER):
                    b, e = divmod(u, SET)
                    done = it * ITER + u
                    sets = it * 2 + b
                    act.wait_ge(up_psum, done + 1)
                    fn(hidden_gate, bank[2 + u % 2][:, 0:P], ACT.Silu).then_inc(silu_done, 1)
                    act.wait_ge(hiddenT_psum, done + 1)
                    fn(hiddenT, bank[4][:, 0:P], ACT.Copy).then_inc(hiddenT_done, 1)
                    if e == 1:
                        act.wait_ge(spread_psum, sets + 1)
                        fn(spread[:, b].rearrange("p t s -> p (t s)"), bank[5][:, :], ACT.Copy
                           ).then_inc(spread_done, 1)
                    act.wait_ge(down_psum, done + 1)
                    for q in range(2):
                        last = fn(y_rows[SLOTS * e:SLOTS * (e + 1), b, q * 256:(q + 1) * 256],
                                  bank[6][SLOTS * q:SLOTS * (q + 1), 0:256], ACT.Copy)
                    last.then_inc(y_done_act, 1)

        @block.vector
        def _(dve):
            ve = nc.vector
            dve.wait_ge(params_in, 16)
            ve.scalar_tensor_tensor(qk_scale, const("q_gain"), DH ** -0.5, const("k_gain"), ALU.mult, ALU.mult
                                    ).then_inc(qk_scale_ready, 1)
            def split_lo(f):
                dve.wait_ge(hi_done, f + 1)
                if f < HALVES:
                    b, half = divmod(f, 2)
                    for c in range(4):
                        hi = w_hi[:, b % 2, 4 * half + c, :]
                        last = ve.scalar_tensor_tensor(
                            w_lo[:, b % 2, 4 * half + c, :], raw[:, half, c * 512:(c + 1) * 512],
                            const("gain_mix")[:, 4 * half + c:4 * half + c + 1], hi.bitcast(F32), ALU.mult,
                            ALU.subtract)
                else:
                    half, quarter = divmod(f - HALVES, 2)
                    chunks = slice(4 * half + 2 * quarter, 4 * half + 2 * quarter + 2)
                    last = ve.tensor_tensor(
                        w_out_lo[:, chunks, :], raw_out[:, half, quarter * 2048:(quarter + 1) * 2048].rearrange(
                            "p (c n) -> p c n", c=2), w_out_hi[:, chunks, :].bitcast(F32), ALU.subtract)
                last.then_inc(split_done, 1)

            for t in range(TILES):
                for half in range(2):
                    dve.wait_ge(hT_hi_done, 2 * t + half + 1)
                    at = (slice(None), slice(4 * half, 4 * half + 4), slice(t * P, (t + 1) * P))
                    ve.tensor_tensor(hT_lo[at], bank[4 + (2 * t + half) % 4][:, :].rearrange("p (c s) -> p c s", c=4),
                                     hT_hi[at].bitcast(F32), ALU.subtract).then_inc(hT_done, 1)
                if t < 2:
                    split_lo(t)
            dve.wait_ge(std_done, 1)
            ve.reciprocal(rstd, std).then_inc(rstd_done, 1)
            dve.wait_ge(rstd_done, 1)

            for u in range(QK_UNITS):
                dve.wait_ge(sq_done, u + 1)
                ve.tensor_reduce(head_ssq[:, u % 2, :], squares.rearrange("p (h d) -> p h d", h=8), AX.X, ALU.add
                                 ).then_inc(hssq_done, 1)
                dve.wait_ge(hstd_done, u + 1)
                ve.reciprocal(head_rstd[:, u % 2, :], head_std[:, u % 2, :]).then_inc(hrstd_done, 1)
                dve.wait_ge(hrstd_done, u + 1)
                ve.tensor_scalar(token_rstd[:, u % 2, :], head_rstd[:, u % 2, :], rstd[:, u % TILES:u % TILES + 1],
                                 None, ALU.mult).then_inc(trstd_done, 1)
                dve.wait_ge(trstd_done, u + 1)
                if u >= 2:
                    dve.wait_ge(qkT_psum, u - 1)
                ve.tensor_tensor(qk_norm[:, u % 2, :].rearrange("p (h d) -> p h d", h=8),
                                 bank[u % 2][:, :].rearrange("p (h d) -> p h d", h=8),
                                 token_rstd[:, u % 2, :, None].to_broadcast([P, 8, DH]), ALU.mult
                                 ).then_inc(qk_normed, 1)
                if u % TILES in (1, 2):
                    split_lo(2 * (u // TILES + 1) + u % TILES - 1)
            for f in range(2 * (BLOCKS - 1), HALVES):
                split_lo(f)

            def mask(n):
                for z in range(2):
                    h, w = 2 * n + z, keys(n)
                    dve.wait_ge(score_done, h + 1)
                    if n >= 3:
                        dve.wait_ge(probT_psum, h - N_PROB + 1)
                    ve.tensor_tensor_reduce(prob[:, h % N_PROB, 0:w], bank[2 * (n % 2) + z][:, 0:w],
                                            const("logmult")[:, SEQ - w:SEQ], -1.0, 3.0e38, ALU.add, ALU.min,
                                            neg_max[:, h:h + 1]).then_inc(masked_done, 1)

            def invert(n):
                dve.wait_ge(exp_done, 2 * n + 2)
                ve.reciprocal(row_inv[:, 2 * n:2 * n + 2], row_sum[:, 2 * n:2 * n + 2]).then_inc(inv_done, 1)

            def store_probT(n):
                dve.wait_ge(probT_psum, 2 * n + 1)
                if n >= 1:
                    dve.wait_ge(attn_psum, n)
                ve.tensor_copy(probT[:, 0, 0:keys(n)], bank[4][:, 0:keys(n)]).then_inc(probT_done[0], 1)

            def store_attn_lo(n):
                i, m = divmod(n, PAIRS)
                dve.wait_ge(attn_hi_done, n + 1)
                if n >= OT_LO:
                    dve.wait_ge(mix_psum, 2 * ((n - OT_LO) // PAIRS + 1))
                ve.tensor_tensor(oT_lo[:, n % OT_LO, :], bank[6][:, 0:P],
                                 oT_hi[:, m, i * P:(i + 1) * P].bitcast(F32), ALU.subtract).then_inc(attn_done, 1)

            def add_mix(i, half):
                dve.wait_ge(mix_psum, 2 * i + half + 1)
                part = resid[:, i, half * 512:(half + 1) * 512]
                ve.tensor_tensor(part, part, bank[7][:, :], ALU.add).then_inc(mix_done, 1)

            def keep_logits(i):
                dve.wait_ge(logit_psum, i + 1)
                ve.tensor_copy(logits[:, i, :], bank[7][:, 0:GROUPS + EXPERTS]).then_inc(logit_done, 1)

            LAG = 3
            for n in range(UNITS + LAG):
                if n < UNITS:
                    mask(n)
                if 1 <= n <= UNITS:
                    invert(n - 1)
                if n >= LAG:
                    store_attn_lo(n - LAG)
                if 2 <= n < UNITS + 2:
                    store_probT(n - 2)
                if n in (3, 4, 5, 6):
                    split_lo(HALVES + n - 3)
                i, step = divmod(n - LAG - PAIRS, PAIRS)
                if i >= 0 and step == 0:
                    add_mix(i, 0)
                    add_mix(i, 1)
                if i >= 0 and step == 3:
                    keep_logits(i)
            add_mix(TILES - 1, 0)
            add_mix(TILES - 1, 1)
            dve.wait_ge(std2_done, 1)
            ve.reciprocal(rstd2, std2).then_inc(rstd2_ready, 1)
            keep_logits(TILES - 1)

            steps = [0]

            def then(instruction):
                steps[0] += 1
                instruction.then_inc(rt_dve, 1)
                dve.wait_ge(rt_dve, steps[0])

            def wide(a, n):
                return a[:, :, None].to_broadcast([P, TILES, n])

            def same(name, n):
                return const(name)[:, None, :].to_broadcast([P, TILES, n])

            n_log = GROUPS + EXPERTS
            dve.wait_ge(logit_done, TILES)
            dve.wait_ge(rstd2_ready, 1)
            then(ve.tensor_tensor(scaled, logits, wide(rstd2, n_log), ALU.mult))
            then(ve.tensor_tensor(scaled, scaled, same("bias", n_log), ALU.add))
            glog = scaled[:, :, 0:GROUPS]
            elog = scaled[:, :, GROUPS:n_log]
            then(ve.tensor_reduce(group_top, glog, AX.X, ALU.max))
            ve.tensor_tensor(group_low, glog, wide(group_top, GROUPS), ALU.subtract).then_inc(low_ready, 1)
            then(ve.tensor_tensor(group_is, glog, wide(group_top, GROUPS), ALU.is_equal))
            then(ve.tensor_tensor(group_val, group_is, same("first8", GROUPS), ALU.mult))
            then(ve.tensor_reduce(group_first, group_val, AX.X, ALU.max))
            then(ve.tensor_tensor(group_is, group_val, wide(group_first, GROUPS), ALU.is_equal))
            then(ve.tensor_scalar(group_val, group_is, -NEVER, NEVER, ALU.mult, ALU.add))
            then(ve.tensor_tensor(cand.rearrange("p t (g e) -> p t g e", g=GROUPS),
                                  elog.rearrange("p t (g e) -> p t g e", g=GROUPS),
                                  group_val[:, :, :, None].to_broadcast([P, TILES, GROUPS, PER_GROUP]), ALU.add))
            for c in range(2):
                then(ve.tensor_reduce(top[c], cand, AX.X, ALU.max))
                then(ve.tensor_tensor(is_top, cand, wide(top[c], EXPERTS), ALU.is_equal))
                then(ve.tensor_tensor(top_val, is_top, same("first64", EXPERTS), ALU.mult))
                then(ve.tensor_reduce(first[c], top_val, AX.X, ALU.max))
                then(ve.tensor_tensor(chosen[c], top_val, wide(first[c], EXPERTS), ALU.is_equal))
                if c == 0:
                    then(ve.scalar_tensor_tensor(cand, chosen[0], 3 * NEVER, cand, ALU.mult, ALU.add))
            ve.tensor_tensor(gap, top[1], top[0], ALU.subtract).then_inc(gap_ready, 1)
            ve.tensor_tensor(picked, chosen[0], chosen[1], ALU.add).then_inc(picked_ready, 1)
            dve.wait_ge(gexp_done, 1)
            then(ve.tensor_reduce(group_sum, group_exp, AX.X, ALU.add))
            then(ve.reciprocal(group_prob, group_sum))
            dve.wait_ge(ratio_done, 1)
            then(ve.tensor_scalar(denom, ratio, 1.0, None, ALU.add))
            then(ve.reciprocal(inv, denom))
            then(ve.tensor_tensor(gate[0], inv, group_prob, ALU.mult))
            then(ve.tensor_tensor(gate[1], gate[0], ratio, ALU.mult))
            then(ve.tensor_tensor(gated, chosen[0], wide(gate[0], EXPERTS), ALU.mult))
            then(ve.tensor_tensor(weight[:, :, 0:EXPERTS], chosen[1], wide(gate[1], EXPERTS), ALU.mult))
            then(ve.tensor_tensor(weight[:, :, 0:EXPERTS], weight[:, :, 0:EXPERTS], gated, ALU.add))
            then(ve.tensor_copy(weight[:, :, EXPERTS:EXPERTS + AHEAD], weight[:, :, 0:AHEAD]))
            dve.wait_ge(rank_psum, 1)
            then(ve.scalar_tensor_tensor(ranked, bank[0][:, 0:TILES * EXPERTS].rearrange("p (t e) -> p t e", t=TILES),
                                         1.0, picked, ALU.add, ALU.mult))
            then(ve.tensor_scalar(rank[:, :, 0:EXPERTS], ranked, -1.0, None, ALU.add))
            then(ve.tensor_scalar(rank[:, :, EXPERTS:EXPERTS + AHEAD], rank[:, :, 0:AHEAD], -float(SLOTS), None,
                                  ALU.add))
            then(ve.tensor_reduce(fullest, bank[1][:, 0:EXPERTS], AX.X, ALU.max))
            then(ve.tensor_scalar(is_round, const("round_start"), fullest, None, ALU.is_lt))
            then(ve.tensor_reduce(rounds_f, is_round, AX.X, ALU.add))
            then(ve.tensor_copy(counts_i[:, 1:2], rounds_f))
            then(ve.tensor_scalar(counts_i[:, 0:1], rounds_f, float(ITERS), None, ALU.mult))
            ve.tensor_copy(slot_now, const("slot")).then_inc(routing_done, 1)
            dve.wait_ge(routing_done, 1)

            dve.sem_inc(added, 1)

            def store_xT(part, b):
                ps = bank[part % 2][:, 0:2 * P]
                ve.tensor_tensor(xT[:, b, 2 * part:2 * part + 2, :], ps.rearrange("p (c s) -> p c s", c=2),
                                 const("gain_ffn_gather")[:, 2 * part:2 * part + 2, None].to_broadcast([P, 2, P]),
                                 ALU.mult).then_inc(xT_done, 1)

            def add_back(t, half, b=7):
                part = resid[:, t, half * 512:(half + 1) * 512]
                return ve.tensor_tensor(part, part, bank[b][:, :], ALU.add)

            def pick_set(b, column):
                ve.tensor_tensor(pick[:, b].rearrange("p t (e s) -> p t e s", e=SET),
                                 slot_now[:, None, None, :].to_broadcast([P, TILES, SET, SLOTS]),
                                 rank[:, :, bass.ds(column, SET)][:, :, :, None].to_broadcast([P, TILES, SET, SLOTS]),
                                 ALU.is_equal).then_inc(pick_done, 1)

            for b in range(2):
                pick_set(b, b * SET)
            for part in range(4):
                dve.wait_ge(gather_psum, part + 1)
                store_xT(part, 0)
            rounds = dve.value_load(counts_i[0:1, 1:2], min_val=1, max_val=MAX_ROUNDS)

            def vector_pass(r, it):
                for u in range(ITER):
                    b, e = divmod(u, SET)
                    done = r * EXPERTS + (it * ITER + u)
                    sets = r * (2 * ITERS) + (it * 2 + b)
                    dve.wait_ge(silu_done, done + 1)
                    ve.tensor_tensor(hidden, hidden_gate, bank[2 + u % 2][:, P:2 * P], ALU.mult
                                     ).then_inc(hidden_done, 1)
                    for half in range(2):
                        dve.wait_ge(combine_psum, done * 2 + half + 1)
                        add_back(e, half).then_inc(added, 1)
                    dve.wait_ge(gather_psum, done + SET + 1)
                    store_xT(e, 1 - b)
                    dve.wait_ge(down_psum, done + 1)
                    for q in range(2, 4):
                        last = ve.tensor_copy(y_rows[SLOTS * e:SLOTS * (e + 1), b, q * 256:(q + 1) * 256],
                                              bank[6][SLOTS * q:SLOTS * (q + 1), 0:256])
                    last.then_inc(y_done_dve, 1)
                    if e == 1:
                        dve.wait_ge(gather_psum, sets * SET + SET)
                        dve.wait_ge(pickg_done, sets + 1)
                        pick_set(b, it * (2 * SET) + (AHEAD + b * SET))

            with dve.Fori(0, rounds) as r:
                with dve.Fori(0, ITERS) as it:
                    vector_pass(r, it)
                dve.wait_ge(pick_done, r * (2 * ITERS) + (2 * ITERS + 2))
                ve.tensor_scalar(slot_now, slot_now, float(SLOTS), None, ALU.add).then_inc(slot_ready, 1)
                dve.wait_ge(slot_ready, r + 1)
            for t in range(TILES):
                for half in range(2):
                    dve.wait_ge(combine_psum, rounds * (2 * EXPERTS) + (2 * t + half + 1))
                    add_back(t, half, 2 * t + half).then_inc(added, 1)

        @block.gpsimd
        def _(pool):
            gp = nc.gpsimd
            gp.memset(ones_bf[:, :], 1.0).then_inc(pool_step, 1)
            pool.wait_ge(pool_step, 1)
            gp.memset(kTz[DH:P, 0], 0.0).then_inc(pool_step, 1)
            pool.wait_ge(pool_step, 2)
            gp.memset(kTz[0:DH, 1], 0.0).then_inc(pool_step, 1)
            pool.wait_ge(pool_step, 3)
            pool.wait_ge(params_in, 16)
            gp.tensor_copy(earlier_bf[:, :], const("earlier")).then_inc(pool_step, 1)
            pool.wait_ge(pool_step, 4)
            pool.wait_ge(router_in, 16)
            gp.tensor_tensor(router, router,
                             const("gain_ffn_router")[:, :, None].to_broadcast([P, CHUNKS, P]), ALU.mult
                             ).then_inc(tables_ready, 1)
            for n in range(UNITS):
                pool.wait_ge(inv_done, n + 1)
                for z in range(2):
                    h, w = 2 * n + z, keys(n)
                    gp.tensor_scalar(prob[:, h % N_PROB, 0:w], prob[:, h % N_PROB, 0:w], row_inv[:, h:h + 1], None,
                                     ALU.mult).then_inc(prob_done, 1)

            pool.wait_ge(low_ready, 1)
            gp.memset(y_rows[:, 1, :], 0.0).then_inc(y_done_dve, 1)
            pool.wait_ge(y_done_dve, 1)
            gp.memset(spread[:, 1], 0.0).then_inc(spread_done, 1)

            def gate_set(b, column):
                gp.tensor_tensor(pick_gated[:, b].rearrange("p t (e s) -> p t e s", e=SET),
                                 pick[:, b].rearrange("p t (e s) -> p t e s", e=SET),
                                 weight[:, :, bass.ds(column, SET)][:, :, :, None].to_broadcast(
                                     [P, TILES, SET, SLOTS]),
                                 ALU.mult).then_inc(pickg_done, 1)

            pool.wait_ge(routing_done, 1)
            rounds = pool.value_load(counts_i[0:1, 1:2], min_val=1, max_val=MAX_ROUNDS)
            for b in range(2):
                pool.wait_ge(pick_done, b + 1)
                gate_set(b, b * SET)
            with pool.Fori(0, rounds) as r:
                with pool.Fori(0, ITERS) as it:
                    for b in range(2):
                        sets = r * (2 * ITERS) + it * 2 + b
                        pool.wait_ge(pick_done, sets + 3)
                        pool.wait_ge(spread_psum, sets + 1)
                        gate_set(b, it * (2 * SET) + (AHEAD + b * SET))


def kernel(**inputs):
    import concourse.bacc as bacc
    from concourse.bass_utils import run_bass_kernel_spmd

    a = {k: np.asarray(v) for k, v in inputs.items()}
    parts = constants()
    per_chunk = lambda g: g.reshape(CHUNKS, P).T
    parts["gain_mix"] = per_chunk(a["norm_mix"][0])
    parts["gain_ffn_router"] = per_chunk(a["norm_ffn"][0])
    parts["gain_ffn_gather"] = a["norm_ffn"][0].reshape(P, CHUNKS)
    parts["q_gain"] = np.tile(a["attn_q_norm"][0], 2)[:, None]
    parts["k_gain"] = np.tile(a["attn_k_norm"][0], 2)[:, None]
    parts["bias"] = np.tile(np.concatenate([a["moe_b_group"][0], a["moe_b_expert"][0]]), (P, 1))
    router = np.zeros((D, P), np.float32)
    router[:, 0:GROUPS] = a["moe_w_group"][0]
    router[:, GROUPS:GROUPS + EXPERTS] = a["moe_w_expert"][0]
    parts["router"] = router.reshape(CHUNKS, P, P).transpose(1, 0, 2).reshape(P, CHUNKS * P)
    params = np.empty((P, PARAMS), np.float32)
    for name, (lo, hi) in COLS.items():
        params[:, lo:hi] = parts[name]

    arrays = dict(x=a["x"][0], params=params, w_in=a["attn_w_in"][0], w_out=a["attn_w_out"][0],
                  w_gate=a["moe_w_gate"][0], w_up=a["moe_w_up"][0], w_down=a["moe_w_down"][0])
    arrays = {k: np.ascontiguousarray(v) for k, v in arrays.items()}
    nc = bacc.Bacc("TRN2", target_bir_lowering=False, num_devices=1)
    args = {k: nc.dram_tensor(k, v.shape, mybir.dt.from_np(v.dtype), kind="ExternalInput").ap()
            for k, v in arrays.items()}
    out = nc.dram_tensor("out", (SEQ, D), F32, kind="ExternalOutput").ap()
    trunk(nc, out=out, **args)
    result = run_bass_kernel_spmd(nc, [arrays], core_ids=[0])
    return result.results[0]["out"].reshape(1, SEQ, D)
```

```python
from contextlib import ExitStack

import numpy as np

import concourse.bass as bass
from concourse import mybir

F32 = mybir.dt.float32
F32R = mybir.dt.float32r
BF16 = mybir.dt.bfloat16
I32 = mybir.dt.int32
ACT = mybir.ActivationFunctionType
ALU = mybir.AluOpType
AX = mybir.AxisListType

P = 128
SEQ, D = 512, 1024
TILES = SEQ // P
CHUNKS = D // P
HEADS, DH = 16, 64
PAIRS = HEADS // 2
BRANCHES = ((128, 1), (512, 4), (2048, 16))
EPS = 1e-6
GROUPS, PER_GROUP = 8, 8
EXPERTS = GROUPS * PER_GROUP
FF = D // 2
FQ = FF // P
SLOTS = 32
SET = P // SLOTS
MAX_ROUNDS = SEQ // SLOTS
NEVER = -1.0e30
PIECE = 4096
RING = 8
LOADS = 3 * RING

_WIDTHS = dict(ident=P, gain_mix=CHUNKS, gain_ffn_gather=CHUNKS, gain_ffn_router=CHUNKS, q_gain=1, k_gain=1, eps=1,
               bias=GROUPS + EXPERTS, first8=GROUPS, first64=EXPERTS, slot=SLOTS, round_start=MAX_ROUNDS, earlier=P,
               logmult=SEQ, router=CHUNKS * P)
COLS, _at = {}, 0
for _name, _w in _WIDTHS.items():
    COLS[_name] = (_at, _at + _w)
    _at += _w
PARAMS = _at
FIRST = COLS["bias"][0]
EARLY = COLS["router"][0]


def matrix_of(n):
    return divmod(n, 3)


LOAD_OF = {matrix_of(n): n for n in range(LOADS)}


def constants():
    d = (SEQ - P) + np.arange(P)[:, None] - np.arange(SEQ)[None, :]
    times = sum(((d >= 0) & (d % dil == 0) & (d <= win)).astype(np.float64) for win, dil in BRANCHES)
    return dict(
        ident=np.eye(P),
        logmult=np.where(times > 0, np.log(np.maximum(times, 1)), NEVER),
        eps=np.full((P, 1), EPS),
        first8=np.tile(GROUPS - np.arange(GROUPS), (P, 1)),
        first64=np.tile(EXPERTS - np.arange(EXPERTS), (P, 1)),
        slot=np.tile(np.arange(SLOTS), (P, 1)),
        round_start=np.tile(SLOTS * np.arange(MAX_ROUNDS), (P, 1)),
        earlier=np.triu(np.ones((P, P)), 1),
    )


def trunk(nc, x, params, w_in, w_out, w_gate, w_up, w_down, out):
    ctx = ExitStack()
    with ctx:
        def sem(name):
            return ctx.enter_context(nc.semaphore(name))

        REGION = 4096
        PAR = -(-PARAMS // 8) * 8
        LOGITS_PAST = 160
        STATISTICS = 6 * TILES + 3 * 16 + 1 + 2 * TILES * HEADS
        SMALL = PAR + 3 * 512 + LOGITS_PAST + STATISTICS
        ring_sb = ctx.enter_context(nc.sbuf_tensor("ring", [P, RING * PIECE], F32))
        regions = ctx.enter_context(nc.sbuf_tensor("regions", [P, 4 * REGION], F32))
        smalls = ctx.enter_context(nc.sbuf_tensor("smalls", [P, SMALL], F32))
        taken = [0]

        def take(n):
            taken[0] += n
            assert taken[0] <= SMALL
            return smalls[:, taken[0] - n:taken[0]]

        ring = ring_sb[:, :].rearrange("p (s n) -> p s n", s=RING)
        region_q = ring[:, RING - 2, :]
        region_v = ring[:, RING - 1, :]
        resid = regions[:, 0:REGION].rearrange("p (t n) -> p t n", t=TILES)
        region_h = regions[:, REGION:2 * REGION]
        region_k = regions[:, 2 * REGION:4 * REGION]
        par_sb = take(PAR)
        scratch_at = taken[0]
        qk_norm = take(2 * 512).rearrange("p (b n) -> p b n", b=2)
        squares = take(512)
        take(LOGITS_PAST)

        def const(name):
            a, b = COLS[name]
            return par_sb[:, a:b]

        ident = const("ident")
        router = const("router").rearrange("p (c n) -> p c n", c=CHUNKS)

        def over(name, memory, at, *shape):
            return nc.alloc_sbuf_tensor_at(name, [P, *shape], F32R, offset=nc.lookup_mloc(memory).addr + 4 * at)

        hT_hi = over("hT_hi", regions, REGION, CHUNKS, SEQ)
        hT_lo = over("hT_lo", ring_sb, 1 * PIECE, CHUNKS, SEQ)
        raw = ring[:, 0, :].rearrange("p (f n) -> p f n", f=2)
        w_hi = over("w_hi", ring_sb, 2 * PIECE, 2, CHUNKS, 512)
        w_lo = over("w_lo", ring_sb, 4 * PIECE, 2, CHUNKS, 512)
        raw_out = ring[:, 0, :].rearrange("p (c n) -> p c n", c=CHUNKS)
        oT_hi = over("oT_hi", ring_sb, (RING - 2) * PIECE, PAIRS, SEQ)
        OT_LO = 11
        oT_lo = over("oT_lo", smalls, scratch_at, OT_LO, P)
        qT = region_q.rearrange("p (m s) -> p m s", m=PAIRS)
        kTz = region_k.rearrange("p (z m s) -> p z m s", z=2, m=PAIRS)
        v = region_v.rearrange("p (b t n) -> p b t n", b=2, t=TILES)
        N_PROB = 6
        prob = region_h[:, 0:N_PROB * 512].rearrange("p (b n) -> p b n", b=N_PROB)
        probT = region_h[:, N_PROB * 512:REGION].rearrange("p (b n) -> p b n", b=2)
        EARLY_UNITS = 2 * TILES - 1
        early_prob = par_sb[:, EARLY:EARLY + N_PROB * P].rearrange("p (b n) -> p b n", b=N_PROB)
        early_probT = par_sb[:, EARLY + N_PROB * P:EARLY + (N_PROB + 2) * P].rearrange("p (b n) -> p b n", b=2)

        def prob_of(h):
            return (early_prob if h < 2 * EARLY_UNITS else prob)[:, h % N_PROB]

        def probT_of(n, z):
            return (early_probT if n < EARLY_UNITS else probT)[:, z]


        h2 = region_h.rearrange("p (t k d) -> p t k d", t=TILES, k=CHUNKS)
        xT = region_k.rearrange("p (b k s) -> p b k s", b=8, k=CHUNKS)[:, 0:2]
        y_rows = region_k.rearrange("p (b n) -> p b n", b=8)[:, 2:4, :]
        pick = region_k.rearrange("p (b t s) -> p b t s", b=16, t=TILES)[:, 8:10]
        pick_gated = region_k.rearrange("p (b t s) -> p b t s", b=16, t=TILES)[:, 10:12]
        spread = region_k.rearrange("p (b t s) -> p b t s", b=16, t=TILES)[:, 12:14]
        hidden_gate = region_k[:, 14 * 512:14 * 512 + P]
        hidden = region_k[:, 14 * 512 + P:14 * 512 + 2 * P]
        hiddenT = region_k[:, 14 * 512 + 2 * P:14 * 512 + 3 * P]

        EARLIEST, OTHERS, GATES = 0, 2, 5
        used = dict.fromkeys((EARLIEST, OTHERS, GATES), 0)

        def rview(*shape, under=OTHERS):
            n = int(np.prod(shape))
            a = region_k[:, under * 1024 + used[under]:under * 1024 + used[under] + n]
            used[under] += n
            assert used[under] <= 1024
            if len(shape) == 2:
                a = a.rearrange("p (a b) -> p a b", a=shape[0])
            return a

        logits_at = scratch_at + OT_LO * P
        logits = smalls[:, logits_at:logits_at + TILES * (GROUPS + EXPERTS)].rearrange("p (t n) -> p t n", t=TILES)
        scaled = rview(TILES, GROUPS + EXPERTS)
        group_top = rview(TILES)
        group_low = rview(TILES, GROUPS)
        group_exp = rview(TILES, GROUPS, under=GATES)
        group_sum = rview(TILES, under=GATES)
        group_prob = rview(TILES, under=GATES)
        group_is = rview(TILES, GROUPS)
        group_val = rview(TILES, GROUPS)
        group_first = rview(TILES)
        cand = rview(TILES, EXPERTS, under=EARLIEST)
        is_top = rview(TILES, EXPERTS, under=EARLIEST)
        top_val = rview(TILES, EXPERTS, under=EARLIEST)
        top = [rview(TILES), rview(TILES)]
        first = [rview(TILES), rview(TILES)]
        chosen = [rview(TILES, EXPERTS, under=GATES), rview(TILES, EXPERTS, under=GATES)]
        gap = rview(TILES, under=GATES)
        ratio = rview(TILES, under=GATES)
        denom = rview(TILES, under=GATES)
        inv = rview(TILES, under=GATES)
        gate = [rview(TILES, under=GATES), rview(TILES, under=GATES)]
        gated = rview(TILES, EXPERTS, under=GATES)
        AHEAD = 2 * SET
        kept = 14 * 512 + 3 * P
        rank = region_k[:, kept:kept + TILES * (EXPERTS + AHEAD)].rearrange("p (t e) -> p t e", t=TILES)
        kept += TILES * (EXPERTS + AHEAD)
        weight = region_k[:, kept:kept + TILES * (EXPERTS + AHEAD)].rearrange("p (t e) -> p t e", t=TILES)
        kept += TILES * (EXPERTS + AHEAD)
        slot_now = region_k[:, kept:kept + SLOTS]
        picked = rview(TILES * EXPERTS // 2, under=GATES).bitcast(BF16).rearrange("p (t e) -> p t e", t=TILES)
        ranked = rview(TILES, EXPERTS)
        fullest = rview(1)
        is_round = rview(MAX_ROUNDS)
        rounds_f = rview(1)
        counts_i = ctx.enter_context(nc.sbuf_tensor("counts_i", [P, 2], I32))
        earlier_bf = ctx.enter_context(nc.sbuf_tensor("earlier_bf", [P, P], BF16))
        ones_bf = ctx.enter_context(nc.sbuf_tensor("ones_bf", [P, P], BF16))

        ssq = take(TILES)
        std = take(TILES)
        rstd = take(TILES)
        ssq2 = take(TILES)
        std2 = take(TILES)
        rstd2 = take(TILES)
        head_ssq = take(16).rearrange("p (b n) -> p b n", b=2)
        head_std = take(16).rearrange("p (b n) -> p b n", b=2)
        head_rstd = take(16).rearrange("p (b n) -> p b n", b=2)
        token_rstd = head_rstd
        qk_scale = take(1)
        neg_max = take(TILES * HEADS)
        row_sum = take(TILES * HEADS)
        row_inv = row_sum

        bank = [ctx.enter_context(nc.psum_tensor(f"bank{i}", [P, 512], F32)) for i in range(8)]

        x_in = [sem(f"x_in{t}") for t in range(TILES)]
        params_in = sem("params_in")
        tables_in = sem("tables_in")
        router_in = sem("router_in")
        raw_in = [sem("raw_in0"), sem("raw_in1")]
        out_raw_in = sem("out_raw_in")
        hi_done = sem("hi_done")
        split_done = sem("split_done")
        first_half_in = sem("first_half_in")
        ring_in = [sem(f"ring_in{s}") for s in range(RING)]
        tables_ready = sem("tables_ready")
        pool_step = sem("pool_step")
        qk_scale_ready = sem("qk_scale_ready")
        ssq_done = sem("ssq_done")
        std_done = sem("std_done")
        rstd_done = sem("rstd_done")
        xT_psum = sem("xT_psum")
        hT_hi_done = sem("hT_hi_done")
        hT_done = sem("hT_done")
        proj_done = sem("proj_done")
        sq_done = sem("sq_done")
        hssq_done = sem("hssq_done")
        hstd_done = sem("hstd_done")
        hrstd_done = sem("hrstd_done")
        trstd_done = sem("trstd_done")
        qk_normed = sem("qk_normed")
        qkT_psum = sem("qkT_psum")
        qkT_done = sem("qkT_done")
        v_done = sem("v_done")
        score_done = sem("score_done")
        masked_done = sem("masked_done")
        exp_done = sem("exp_done")
        inv_done = sem("inv_done")
        prob_done = sem("prob_done")
        probT_psum = sem("probT_psum")
        probT_done = [sem("probT_done_even"), sem("probT_done_odd")]
        attn_psum = sem("attn_psum")
        attn_hi_done = sem("attn_hi_done")
        attn_done = sem("attn_done")
        mix_psum = sem("mix_psum")
        mix_first = sem("mix_first")
        mix_done = sem("mix_done")
        ssq2_done = sem("ssq2_done")
        x2T_psum = sem("x2T_psum")
        x2T_done = sem("x2T_done")
        logit_psum = sem("logit_psum")
        logit_done = sem("logit_done")
        rt_dve = sem("rt_dve")
        std2_done = sem("std2_done")
        rstd2_ready = sem("rstd2_ready")
        low_ready = sem("low_ready")
        gexp_done = sem("gexp_done")
        gap_ready = sem("gap_ready")
        ratio_done = sem("ratio_done")
        picked_ready = sem("picked_ready")
        rank_psum = sem("rank_psum")
        routing_done = sem("routing_done")
        h2_done = sem("h2_done")
        slot_ready = sem("slot_ready")
        pick_first = sem("pick_first")
        pick_done = sem("pick_done")
        gates_ready = sem("gates_ready")
        pickg_done = sem("pickg_done")
        gather_psum = sem("gather_psum")
        xT_done = sem("xT_done")
        gate_psum = sem("gate_psum")
        up_psum = sem("up_psum")
        silu_done = sem("silu_done")
        hidden_done = sem("hidden_done")
        hiddenT_psum = sem("hiddenT_psum")
        hiddenT_done = sem("hiddenT_done")
        spread_psum = sem("spread_psum")
        spread_done = sem("spread_done")
        down_psum = sem("down_psum")
        y_done_act = sem("y_done_act")
        y_done_dve = sem("y_done_dve")
        combine_psum = sem("combine_psum")
        added = sem("added")
        out_stored = sem("out_stored")

        BLOCKS = 6
        QK_UNITS = 4 * TILES
        UNITS = TILES * PAIRS
        ITER = 2 * SET
        ITERS = EXPERTS // ITER
        COMBINE_BANK = (7, 5)
        LAG = 3

        V_NEEDED = {0: 1, PAIRS // 2: TILES + 1}
        V_NEEDED.update({t * PAIRS: TILES + t + 1 for t in range(1, TILES)})
        W_OUT_PARTS = 8

        W_OUT_STEP = (3, 3, 4, 4, PAIRS, PAIRS + 2, PAIRS + 3, PAIRS + 4)

        LAST_MIX = {UNITS - 1: (1, range(4)), UNITS: (1, range(4, 5)), UNITS + 1: (1, range(5, 6)),
                    UNITS + 2: (0, range(4))}

        def final_bank(t, half):
            return (2 * t + half + 2) % 8

        def mix_bank(i, half):
            return 0 if i == TILES - 1 and half == 1 else 7

        def x2T_bank(i, half):
            return 6 if i == TILES - 1 and half == 1 else 7

        def keys(n):
            return (n // PAIRS + 1) * P

        gate_v = w_gate.rearrange("e (p k) n -> e p (k n)", k=CHUNKS)
        up_v = w_up.rearrange("e (p k) n -> e p (k n)", k=CHUNKS)
        down_v = w_down.rearrange("e (j p) n -> e p j n", p=P)
        HALVES = 2 * BLOCKS
        W_IN_PARTS = 2 * HALVES

        block = ctx.enter_context(nc.Block())

        @block.sync
        def _(sp):
            def load_x(t):
                sp.dma_start(resid[:, t, :], x[t * P:(t + 1) * P, :]).then_inc(x_in[t], 16)

            def load_w_in(f):
                b, half = divmod(f, 2)
                if f >= 2:
                    sp.wait_ge(split_done, 2 * (f - 1))
                sp.dma_start(raw[:, half, :].rearrange("p (c n) -> p c n", c=4),
                             w_in[half * 512:(half + 1) * 512, b * 512:(b + 1) * 512].rearrange(
                                 "(c p) n -> p c n", p=P)).then_inc(raw_in[half], 16)

            sp.dma_start(par_sb[:, 0:FIRST], params[:, 0:FIRST]).then_inc(params_in, 16)
            load_x(0)
            load_w_in(0)
            load_x(1)
            load_w_in(1)
            load_x(2)
            load_x(3)
            sp.dma_start(par_sb[:, FIRST:EARLY], params[:, FIRST:EARLY]).then_inc(tables_in, 16)
            for f in range(2, HALVES):
                load_w_in(f)
            for half in range(2):
                sp.wait_ge(split_done, W_IN_PARTS + 4 * half)
                sp.dma_start(raw_out, w_out[:, half * 512:(half + 1) * 512].rearrange("(c p) n -> p c n", p=P)
                             ).then_inc(out_raw_in, 16)
            sp.wait_ge(attn_psum, EARLY_UNITS)
            sp.dma_start(par_sb[:, EARLY:PARAMS], params[:, EARLY:PARAMS]).then_inc(router_in, 16)

            def load(n, first_expert):
                e, what = matrix_of(n)
                piece, expert = ring[:, n % RING, :], first_expert + e
                if what == 2:
                    sp.dma_start(piece.rearrange("p (j n) -> p j n", j=FQ), down_v[expert]
                                 ).then_inc(ring_in[n % RING], 16)
                else:
                    sp.dma_start(piece, (gate_v, up_v)[what][expert]).then_inc(ring_in[n % RING], 16)

            def load_half(n, half):
                e, what = matrix_of(n)
                columns = slice(half * (PIECE // 2), (half + 1) * (PIECE // 2))
                piece = ring[:, n % RING, columns]
                signal = ring_in[n % RING] if half == 1 else first_half_in
                if what == 2:
                    sp.dma_start(piece.rearrange("p (j n) -> p j n", j=FQ // 2),
                                 down_v[e][:, 2 * half:2 * half + 2, :]).then_inc(signal, 16)
                else:
                    sp.dma_start(piece, (gate_v, up_v)[what][e][:, columns]).then_inc(signal, 16)

            def wait_used(n, experts_before):
                e, what = matrix_of((n - RING) % LOADS)
                if n < RING:
                    e -= RING
                sp.wait_ge((gate_psum, up_psum, down_psum)[what], experts_before + (e + 1))

            sp.wait_ge(proj_done, BLOCKS * TILES)
            load(1, 0)
            sp.wait_ge(split_done, W_IN_PARTS + W_OUT_PARTS)
            load(0, 0)
            sp.wait_ge(attn_psum, UNITS - PAIRS // 2)
            load_half(RING - 1, 0)
            sp.wait_ge(mix_first, 1)
            load_half(3, 0)
            load_half(5, 0)
            sp.wait_ge(attn_psum, UNITS)
            load_half(RING - 1, 1)
            sp.wait_ge(mix_first, 2)
            load_half(2, 0)
            load_half(4, 0)
            for half in range(2):
                sp.wait_ge(mix_psum, 2 * TILES - 1 + half)
                load_half(2 + half, 1)
                load_half(4 + half, 1)
            sp.wait_ge(logit_psum, TILES)
            sp.wait_ge(ssq2_done, TILES)
            load(RING - 2, 0)
            for n in range(RING, LOADS):
                wait_used(n, 0)
                load(n, 0)
            with sp.Fori(1, EXPERTS // RING) as turn:
                for n in range(LOADS):
                    wait_used(n, turn * RING)
                    load(n, turn * RING)
            sp.wait_ge(routing_done, 1)
            rounds = sp.value_load(counts_i[0:1, 1:2], min_val=1, max_val=MAX_ROUNDS)
            with sp.If(rounds > 1):
                with sp.Fori(1, rounds) as r:
                    with sp.Fori(0, EXPERTS // RING) as turn:
                        for n in range(LOADS):
                            wait_used(n, r * EXPERTS + turn * RING)
                            load(n, turn * RING)
            for t in range(TILES):
                sp.wait_ge(added, rounds * (2 * EXPERTS) + (2 * t + 4))
                sp.dma_start(out[t * P:(t + 1) * P, :], resid[:, t, :]).then_inc(out_stored, 16)
            sp.wait_ge(out_stored, 16 * TILES)

        @block.tensor
        def _(pe):
            mm, tr = nc.tensor.matmul, nc.tensor.transpose
            pe.wait_ge(params_in, 16)

            def turn_x(t):
                pe.wait_ge(x_in[t], 16)
                for half in range(2):
                    b = 4 + (2 * t + half) % 4
                    if t >= 2:
                        pe.wait_ge(hT_done, 2 * (t - 2) + half + 1)
                    for c in range(4):
                        last = tr(bank[b][:, c * P:(c + 1) * P],
                                  resid[:, t, (4 * half + c) * P:(4 * half + c + 1) * P], ident)
                    last.then_inc(xT_psum, 1)

            def split_product(out, hi, lo, w_hi_c, w_lo_c, first, final):
                mm(out, hi, w_hi_c, start=first, stop=False)
                mm(out, hi, w_lo_c, start=False, stop=False)
                return mm(out, lo, w_hi_c, start=False, stop=final)

            def project(u):
                b, t = divmod(u, TILES)
                if u < TILES:
                    pe.wait_ge(hT_done, 2 * (t + 1))
                if 2 <= u < QK_UNITS:
                    pe.wait_ge(qk_normed, u - 1)
                elif u > QK_UNITS:
                    pe.wait_ge(v_done, u - QK_UNITS)
                for c in range(CHUNKS):
                    if t == 0 and c % 2 == 0:
                        pe.wait_ge(split_done, 4 * b + c // 2 + 1)
                    last = split_product(bank[u % 2 if u < QK_UNITS else 7][:, :], hT_hi[:, c, t * P:(t + 1) * P],
                                         hT_lo[:, c, t * P:(t + 1) * P], w_hi[:, b % 2, c, :], w_lo[:, b % 2, c, :],
                                         c == 0, c == CHUNKS - 1)
                last.then_inc(proj_done, 1)

            def turn_qk(u):
                pe.wait_ge(qk_normed, u + 1)
                if u >= 2:
                    pe.wait_ge(qkT_done, u - 1)
                for c in range(4):
                    last = tr(bank[2 + u % 2][:, c * P:(c + 1) * P], qk_norm[:, u % 2, c * P:(c + 1) * P], ident)
                last.then_inc(qkT_psum, 1)

            for u in range(QK_UNITS + 1):
                if u < 2:
                    turn_x(2 * u)
                    turn_x(2 * u + 1)
                project(u)
                if u >= 1:
                    turn_qk(u - 1)

            def scores(n):
                i, m = divmod(n, PAIRS)
                if n == 0:
                    pe.wait_ge(qk_normed, QK_UNITS)
                    pe.wait_ge(qkT_done, QK_UNITS - TILES + 1)
                elif n == 1:
                    pe.wait_ge(qkT_done, QK_UNITS)
                for z in range(2):
                    if n >= 2:
                        pe.wait_ge(masked_done, 2 * (n - 2) + z + 1)
                    mm(bank[2 * (n % 2) + z][:, 0:keys(n)], qT[:, m, i * P:(i + 1) * P], kTz[:, z, m, 0:keys(n)],
                       start=True, stop=True).then_inc(score_done, 1)

            def turn_probs(n):
                for z in range(2):
                    pe.wait_ge(prob_done, 2 * n + z + 1)
                    if n >= 1:
                        pe.wait_ge(probT_done[z], n)
                    for kb in range(n // PAIRS + 1):
                        last = tr(bank[4 + z][:, kb * P:(kb + 1) * P],
                                  prob_of(2 * n + z)[:, kb * P:(kb + 1) * P], ident)
                    last.then_inc(probT_psum, 1)

            def attend(n):
                i, m = divmod(n, PAIRS)
                pe.wait_ge(probT_done[0], n + 1)
                pe.wait_ge(probT_done[1], n + 1)
                if n >= 1:
                    pe.wait_ge(attn_done, n)
                if n in V_NEEDED:
                    pe.wait_ge(v_done, V_NEEDED[n])
                for kb in range(i + 1):
                    for z in range(2):
                        last = mm(bank[6][z * DH:(z + 1) * DH, 0:P],
                                  v[:, m // 4, kb, (2 * m % 8 + z) * DH:(2 * m % 8 + z + 1) * DH],
                                  probT_of(n, z)[:, kb * P:(kb + 1) * P],
                                  start=(kb == 0), stop=(kb == i))
                last.then_inc(attn_psum, 1)

            def mix(i, half, chunks=range(CHUNKS)):
                first, final = chunks[0] == 0, chunks[-1] == CHUNKS - 1
                pe.wait_ge(attn_done, PAIRS * i + chunks[-1] + 1)
                if i == 0:
                    pe.wait_ge(split_done, W_IN_PARTS + 4 * half + chunks[-1] // 2 + 1)
                if first and i == TILES - 1 and half == 1:
                    pe.wait_ge(masked_done, 2 * UNITS - 3)
                elif first and half == 1:
                    pe.wait_ge(mix_done, 2 * i + 1)
                elif first and i >= 1:
                    pe.wait_ge(logit_done, i)
                for c in chunks:
                    last = split_product(bank[mix_bank(i, half)][:, :], oT_hi[:, c, i * P:(i + 1) * P],
                                         oT_lo[:, (PAIRS * i + c) % OT_LO, :], w_hi[:, half, c, :],
                                         w_lo[:, half, c, :], c == 0, c == CHUNKS - 1)
                if final:
                    last.then_inc(mix_psum, 1)
                elif first and i == TILES - 1:
                    last.then_inc(mix_first, 1)

            def turn_x2(i, half):
                pe.wait_ge(mix_done, 2 * (i + 1))
                if half == 1 and i < TILES - 1:
                    pe.wait_ge(x2T_done, 2 * i + 1)
                for c in range(4):
                    last = tr(bank[x2T_bank(i, half)][:, c * P:(c + 1) * P],
                              resid[:, i, (4 * half + c) * P:(4 * half + c + 1) * P], ident)
                last.then_inc(x2T_psum, 1)

            def route(i):
                pe.wait_ge(x2T_done, 2 * i + 1 if i == TILES - 1 else 2 * (i + 1))
                pe.wait_ge(tables_ready, 1)
                for c in range(CHUNKS):
                    if i == TILES - 1 and c == 4:
                        pe.wait_ge(x2T_done, 2 * TILES)
                    last = mm(bank[7][:, 0:P], qT[:, c, i * P:(i + 1) * P], router[:, c, :],
                              start=(c == 0), stop=(c == CHUNKS - 1))
                last.then_inc(logit_psum, 1)

            def tail(i, step):
                if step < 4:
                    mix(i, step // 2, range(4 * (step % 2), 4 * (step % 2) + 4))
                elif step < 6:
                    turn_x2(i, step - 4)
                elif step == 6:
                    route(i)

            for n in range(UNITS + LAG):
                if n < UNITS:
                    scores(n)
                if n >= LAG:
                    attend(n - LAG)
                if 2 <= n < UNITS + 2:
                    turn_probs(n - 2)
                i, step = divmod(n - LAG - PAIRS, PAIRS)
                if n < EARLY_UNITS:
                    project(QK_UNITS + 1 + n)
                if n == EARLY_UNITS + 1:
                    mix(0, 0, range(4))
                elif i > 0 or i == 0 and step > 0:
                    tail(i, step)
                if n in LAST_MIX:
                    mix(TILES - 1, *LAST_MIX[n])
            mix(TILES - 1, 0, range(4, CHUNKS - 1))
            mix(TILES - 1, 1, range(CHUNKS - 2, CHUNKS - 1))
            mix(TILES - 1, 0, range(CHUNKS - 1, CHUNKS))
            mix(TILES - 1, 1, range(CHUNKS - 1, CHUNKS))

            def ranks(tiles):
                for t in tiles:
                    for s in range(t + 1):
                        last = mm(bank[2][:, t * EXPERTS:(t + 1) * EXPERTS],
                                  earlier_bf[:, :] if s == t else ones_bf[:, :], picked[:, s, :],
                                  start=(s == 0), stop=(s == t))
                return last

            def gather_first(tiles):
                for c in range(CHUNKS):
                    for t in tiles:
                        last = mm(bank[c // 4][:, c % 4 * P:(c % 4 + 1) * P], h2[:, t, c, :], pick[:, 0, t, :],
                                  start=(t == 0 and c % 4 == 0), stop=(t == TILES - 1 and c % 4 == 3))
                    if c % 4 == 3 and tiles[-1] == TILES - 1:
                        last.then_inc(gather_psum, 2)

            turn_x2(TILES - 1, 0)
            turn_x2(TILES - 1, 1)
            pe.wait_ge(tables_ready, 1)
            pe.wait_ge(masked_done, 2 * UNITS)
            pe.wait_ge(picked_ready, 1)
            ranks(range(TILES - 1)).then_inc(rank_psum, 1)
            route(TILES - 1)
            pe.wait_ge(h2_done, TILES - 1)
            pe.wait_ge(pick_first, 1)
            gather_first(range(TILES - 1))
            pe.wait_ge(picked_ready, 2)
            ranks(range(TILES - 1, TILES))
            for t in range(TILES):
                last = mm(bank[3][:, 0:EXPERTS], ones_bf[:, :], picked[:, t, :], start=(t == 0), stop=(t == TILES - 1))
            last.then_inc(rank_psum, 1)
            pe.wait_ge(h2_done, TILES)
            pe.wait_ge(pick_done, 1)
            gather_first(range(TILES - 1, TILES))

            def gather(part, picks):
                b = part % 2
                for c in range(2):
                    for t in range(TILES):
                        last = mm(bank[b][:, c * P:(c + 1) * P], h2[:, t, 2 * part + c, :],
                                  picks[:, t, :], start=(t == 0), stop=(t == TILES - 1))
                last.then_inc(gather_psum, 1)

            def combine(t, half, b, to):
                return mm(bank[to][:, :], spread[:, b, t, :], y_rows[:, b, half * 512:(half + 1) * 512],
                          start=True, stop=True).then_inc(combine_psum, 1)

            pe.wait_ge(routing_done, 1)
            passes = pe.value_load(counts_i[0:1, 0:1], min_val=ITERS, max_val=ITERS * MAX_ROUNDS)
            pe.wait_ge(first_half_in, 5 * 16)
            with pe.Fori(0, passes) as it:
                for u in range(ITER):
                    b, e = divmod(u, SET)
                    done = it * ITER + u
                    sets = it * 2 + b
                    n_gate, n_up, n_down = (LOAD_OF[u, what] for what in range(3))
                    if e == 0:
                        pe.wait_ge(y_done_act, done + 1)
                        pe.wait_ge(y_done_dve, done + 1)
                        pe.wait_ge(spread_done, sets + 1)
                    for half in range(2):
                        if e == 2 and half == 1:
                            pe.wait_ge(spread_done, sets + 2)
                        pe.wait_ge(added, done * 2 + (half + 1))
                        combine(e, half, 1 - b, to=COMBINE_BANK[half])
                    if e == 0:
                        pe.wait_ge(xT_done, done + SET)
                    for what, n in enumerate((n_gate, n_up)):
                        pe.wait_ge(ring_in[n % RING], it * (16 * LOADS // RING) + 16 * (n // RING + 1))
                        for k in range(CHUNKS):
                            for j in range(FQ):
                                last = mm(bank[2 + u % 2][SLOTS * j:SLOTS * (j + 1), what * P:(what + 1) * P],
                                          xT[:, b, k, SLOTS * e:SLOTS * (e + 1)],
                                          ring[:, n % RING, k * FF + j * P:k * FF + (j + 1) * P],
                                          start=(k == 0), stop=(k == CHUNKS - 1))
                        last.then_inc((gate_psum, up_psum)[what], 1)
                    pe.wait_ge(hidden_done, done + 1)
                    tr(bank[4][:, 0:P], hidden, ident).then_inc(hiddenT_psum, 1)
                    if e == 1:
                        pe.wait_ge(pickg_done, sets + 1)
                        pe.wait_ge(added, done * 2 + 4)
                        for t in range(TILES):
                            last = tr(bank[5][:, t * P:(t + 1) * P], pick_gated[:, b, t, :], ident)
                        last.then_inc(spread_psum, 1)
                    pe.wait_ge(hiddenT_done, done + 1)
                    pe.wait_ge(ring_in[n_down % RING], it * (16 * LOADS // RING) + 16 * (n_down // RING + 1))
                    pe.wait_ge(y_done_act, done + 1)
                    pe.wait_ge(y_done_dve, done + 1)
                    for j in range(FQ):
                        for q in range(4):
                            last = mm(bank[6][SLOTS * q:SLOTS * (q + 1), 0:256], hiddenT[:, SLOTS * j:SLOTS * (j + 1)],
                                      ring[:, n_down % RING, j * D + q * 256:j * D + (q + 1) * 256],
                                      start=(j == 0), stop=(j == FQ - 1))
                    last.then_inc(down_psum, 1)
                    if e == 0:
                        pe.wait_ge(pick_done, sets + 2)
                    pe.wait_ge(xT_done, done + 3)
                    gather(e, pick[:, 1 - b])
            pe.wait_ge(y_done_act, passes * ITER + 1)
            pe.wait_ge(y_done_dve, passes * ITER + 1)
            pe.wait_ge(spread_done, passes * 2 + 1)
            pe.wait_ge(added, passes * (2 * ITER) + 2)
            for t in range(TILES):
                if t == TILES - 1:
                    pe.wait_ge(xT_done, passes * ITER + SET)
                for half in range(2):
                    combine(t, half, 1, to=final_bank(t, half))

        @block.scalar
        def _(act):
            fn = nc.scalar.activation
            act.wait_ge(params_in, 16)
            def split_hi(f):
                if f < HALVES:
                    b, half = divmod(f, 2)
                    act.wait_ge(raw_in[half], 16 * (b + 1))
                    if b >= 2:
                        act.wait_ge(proj_done, TILES * (b - 1))
                    for c in range(4):
                        last = fn(w_hi[:, b % 2, 4 * half + c, :], raw[:, half, c * 512:(c + 1) * 512], ACT.Copy,
                                  scale=const("gain_mix")[:, 4 * half + c:4 * half + c + 1])
                        if c == 1:
                            last.then_inc(hi_done, 1)
                else:
                    half, part = divmod(f - HALVES, 4)
                    act.wait_ge(out_raw_in, 16 * (half + 1))
                    act.wait_ge(proj_done, TILES * (BLOCKS - 1 + half))
                    chunks = slice(2 * part, 2 * part + 2)
                    last = fn(w_hi[:, half, chunks, :], raw_out[:, chunks, :], ACT.Copy)
                last.then_inc(hi_done, 1)

            def store_hT_hi(t):
                for half in range(2):
                    act.wait_ge(xT_psum, 2 * t + half + 1)
                    fn(hT_hi[:, 4 * half:4 * half + 4, t * P:(t + 1) * P],
                       bank[4 + (2 * t + half) % 4][:, :].rearrange("p (c s) -> p c s", c=4), ACT.Copy
                       ).then_inc(hT_hi_done, 1)

            for t in range(2):
                store_hT_hi(t)
                split_hi(t)
            for t in range(TILES):
                act.wait_ge(x_in[t], 16)
                fn(region_q[:, t * D:(t + 1) * D], resid[:, t, :], ACT.Square,
                   accum_out=ssq[:, t:t + 1]).then_inc(ssq_done, 1)
            act.wait_ge(ssq_done, TILES)
            fn(std, ssq, ACT.Sqrt, bias=const("eps"), scale=1.0 / D).then_inc(std_done, 1)
            for t in range(2, TILES):
                store_hT_hi(t)

            def store_qk(u):
                b, t = divmod(u, TILES)
                act.wait_ge(qkT_psum, u + 1)
                src = bank[2 + u % 2][:, :].rearrange("p (m s) -> p m s", m=4)
                pairs, toks = slice(4 * (b % 2), 4 * (b % 2) + 4), slice(t * P, (t + 1) * P)
                if b < 2:
                    fn(qT[:, pairs, toks], src, ACT.Copy, scale=qk_scale).then_inc(qkT_done, 1)
                else:
                    fn(kTz[0:DH, 0, pairs, toks], src[0:DH], ACT.Copy)
                    fn(kTz[DH:P, 1, pairs, toks], src[DH:P], ACT.Copy).then_inc(qkT_done, 1)

            act.wait_ge(qk_scale_ready, 1)
            act.wait_ge(pool_step, 3)
            act.wait_ge(rstd_done, 1)
            for u in range(QK_UNITS):
                act.wait_ge(proj_done, u + 1)
                if u >= 1:
                    act.wait_ge(hssq_done, u)
                fn(squares, bank[u % 2][:, :], ACT.Square, scale=rstd[:, u % TILES:u % TILES + 1]
                   ).then_inc(sq_done, 1)
                act.wait_ge(hssq_done, u + 1)
                fn(head_std[:, u % 2, :], head_ssq[:, u % 2, :], ACT.Sqrt, bias=const("eps"),
                   scale=1.0 / DH).then_inc(hstd_done, 1)
                if u >= 1:
                    store_qk(u - 1)
                if u % TILES in (1, 2):
                    split_hi(2 * (u // TILES + 1) + u % TILES - 1)
            def store_v(j):
                b, t = divmod(j, TILES)
                act.wait_ge(proj_done, QK_UNITS + j + 1)
                fn(v[:, b, t, :], bank[7][:, :], ACT.Copy, scale=rstd[:, t:t + 1]
                   ).then_inc(v_done, 1)

            store_v(0)
            store_qk(QK_UNITS - 1)

            def exponent(n):
                for z in range(2):
                    h, w = 2 * n + z, keys(n)
                    act.wait_ge(masked_done, h + 1)
                    fn(prob_of(h)[:, 0:w], prob_of(h)[:, 0:w], ACT.Exp, scale=-1.0,
                       bias=neg_max[:, h:h + 1], accum_out=row_sum[:, h:h + 1]).then_inc(exp_done, 1)

            def store_probT(n):
                act.wait_ge(probT_psum, 2 * n + 2)
                if n >= 1:
                    act.wait_ge(attn_psum, n)
                fn(probT_of(n, 1)[:, 0:keys(n)], bank[5][:, 0:keys(n)], ACT.Copy).then_inc(probT_done[1], 1)

            def store_attn(n):
                i, m = divmod(n, PAIRS)
                act.wait_ge(attn_psum, n + 1)
                fn(oT_hi[:, m, i * P:(i + 1) * P], bank[6][:, 0:P], ACT.Copy).then_inc(attn_hi_done, 1)

            def store_x2T(i, half):
                act.wait_ge(x2T_psum, 2 * i + half + 1)
                fn(qT[:, 4 * half:4 * half + 4, i * P:(i + 1) * P],
                   bank[x2T_bank(i, half)][:, :].rearrange("p (c s) -> p c s", c=4), ACT.Copy).then_inc(x2T_done, 1)

            def square_x2(i):
                act.wait_ge(mix_done, 2 * (i + 1))
                j = max(i - 1, 0)
                act.wait_ge(logit_psum, j + 1)
                fn(qT[:, :, j * P:(j + 1) * P], resid[:, i, :].rearrange("p (c s) -> p c s", c=CHUNKS),
                   ACT.Square, accum_out=ssq2[:, i:i + 1]).then_inc(ssq2_done, 1)

            def root_x2(tiles):
                act.wait_ge(ssq2_done, tiles.stop)
                fn(std2[:, tiles], ssq2[:, tiles], ACT.Sqrt, bias=const("eps"), scale=1.0 / D).then_inc(std2_done, 1)

            for n in range(UNITS + LAG):
                if n < UNITS:
                    exponent(n)
                if n >= LAG:
                    store_attn(n - LAG)
                if 2 <= n < UNITS + 2:
                    store_probT(n - 2)
                i, step = divmod(n - LAG - PAIRS, PAIRS)
                if n < EARLY_UNITS:
                    store_v(n + 1)
                if n < 2:
                    split_hi(HALVES - 2 + n)
                for g in range(W_OUT_PARTS):
                    if W_OUT_STEP[g] == n:
                        split_hi(HALVES + g)
                if i >= 0 and step in (4, 5):
                    store_x2T(i, step - 4)
                if i >= 0 and step == 6:
                    square_x2(i)
                if n == UNITS + 1:
                    root_x2(slice(0, TILES - 1))
            def rows_for_gather(t):
                fn(h2[:, t], resid[:, t, :].rearrange("p (d k) -> p k d", k=CHUNKS), ACT.Copy,
                   scale=rstd2[:, t:t + 1]).then_inc(h2_done, 1)

            act.wait_ge(rstd2_ready, 1)
            for t in range(TILES - 1):
                rows_for_gather(t)
            store_x2T(TILES - 1, 0)
            store_x2T(TILES - 1, 1)
            square_x2(TILES - 1)
            root_x2(slice(TILES - 1, TILES))
            act.wait_ge(rstd2_ready, 2)
            rows_for_gather(TILES - 1)
            act.wait_ge(low_ready, 2)
            fn(group_exp, group_low, ACT.Exp).then_inc(gexp_done, 1)
            act.wait_ge(gap_ready, 1)
            fn(ratio, gap, ACT.Exp).then_inc(ratio_done, 1)

            act.wait_ge(routing_done, 1)
            passes = act.value_load(counts_i[0:1, 0:1], min_val=ITERS, max_val=ITERS * MAX_ROUNDS)
            act.sem_inc(y_done_act, 1)
            with act.Fori(0, passes) as it:
                for u in range(ITER):
                    b, e = divmod(u, SET)
                    done = it * ITER + u
                    sets = it * 2 + b
                    act.wait_ge(up_psum, done + 1)
                    fn(hidden_gate, bank[2 + u % 2][:, 0:P], ACT.Silu).then_inc(silu_done, 1)
                    act.wait_ge(hiddenT_psum, done + 1)
                    fn(hiddenT, bank[4][:, 0:P], ACT.Copy).then_inc(hiddenT_done, 1)
                    if e == 1:
                        act.wait_ge(spread_psum, sets + 1)
                        fn(spread[:, b].rearrange("p t s -> p (t s)"), bank[5][:, :], ACT.Copy
                           ).then_inc(spread_done, 1)
                    act.wait_ge(down_psum, done + 1)
                    for q in range(2):
                        last = fn(y_rows[SLOTS * e:SLOTS * (e + 1), b, q * 256:(q + 1) * 256],
                                  bank[6][SLOTS * q:SLOTS * (q + 1), 0:256], ACT.Copy)
                    last.then_inc(y_done_act, 1)

        @block.vector
        def _(dve):
            ve = nc.vector
            dve.wait_ge(params_in, 16)
            ve.scalar_tensor_tensor(qk_scale, const("q_gain"), DH ** -0.5, const("k_gain"), ALU.mult, ALU.mult
                                    ).then_inc(qk_scale_ready, 1)
            def split_lo(f):
                if f < HALVES:
                    b, half = divmod(f, 2)
                    for c in range(4):
                        if c % 2 == 0:
                            dve.wait_ge(hi_done, 2 * f + c // 2 + 1)
                        hi = w_hi[:, b % 2, 4 * half + c, :]
                        last = ve.scalar_tensor_tensor(
                            w_lo[:, b % 2, 4 * half + c, :], raw[:, half, c * 512:(c + 1) * 512],
                            const("gain_mix")[:, 4 * half + c:4 * half + c + 1], hi.bitcast(F32), ALU.mult,
                            ALU.subtract)
                        if c == 1:
                            last.then_inc(split_done, 1)
                else:
                    dve.wait_ge(hi_done, f - HALVES + W_IN_PARTS + 1)
                    half, part = divmod(f - HALVES, 4)
                    chunks = slice(2 * part, 2 * part + 2)
                    last = ve.tensor_tensor(w_lo[:, half, chunks, :], raw_out[:, chunks, :],
                                            w_hi[:, half, chunks, :].bitcast(F32), ALU.subtract)
                last.then_inc(split_done, 1)

            for t in range(TILES):
                for half in range(2):
                    dve.wait_ge(hT_hi_done, 2 * t + half + 1)
                    at = (slice(None), slice(4 * half, 4 * half + 4), slice(t * P, (t + 1) * P))
                    ve.tensor_tensor(hT_lo[at], bank[4 + (2 * t + half) % 4][:, :].rearrange("p (c s) -> p c s", c=4),
                                     hT_hi[at].bitcast(F32), ALU.subtract).then_inc(hT_done, 1)
                if t < 2:
                    split_lo(t)
            dve.wait_ge(std_done, 1)
            ve.reciprocal(rstd, std).then_inc(rstd_done, 1)
            dve.wait_ge(rstd_done, 1)

            for u in range(QK_UNITS):
                dve.wait_ge(sq_done, u + 1)
                ve.tensor_reduce(head_ssq[:, u % 2, :], squares.rearrange("p (h d) -> p h d", h=8), AX.X, ALU.add
                                 ).then_inc(hssq_done, 1)
                dve.wait_ge(hstd_done, u + 1)
                ve.reciprocal(head_rstd[:, u % 2, :], head_std[:, u % 2, :]).then_inc(hrstd_done, 1)
                dve.wait_ge(hrstd_done, u + 1)
                ve.tensor_scalar(token_rstd[:, u % 2, :], head_rstd[:, u % 2, :], rstd[:, u % TILES:u % TILES + 1],
                                 None, ALU.mult).then_inc(trstd_done, 1)
                dve.wait_ge(trstd_done, u + 1)
                if u >= 2:
                    dve.wait_ge(qkT_psum, u - 1)
                ve.tensor_tensor(qk_norm[:, u % 2, :].rearrange("p (h d) -> p h d", h=8),
                                 bank[u % 2][:, :].rearrange("p (h d) -> p h d", h=8),
                                 token_rstd[:, u % 2, :, None].to_broadcast([P, 8, DH]), ALU.mult
                                 ).then_inc(qk_normed, 1)
                if u % TILES in (1, 2):
                    split_lo(2 * (u // TILES + 1) + u % TILES - 1)

            def mask(n):
                for z in range(2):
                    h, w = 2 * n + z, keys(n)
                    if h == 0:
                        dve.wait_ge(tables_in, 16)
                    if h == 2 * EARLY_UNITS:
                        dve.wait_ge(proj_done, BLOCKS * TILES)
                    dve.wait_ge(score_done, h + 1)
                    if n >= 3:
                        dve.wait_ge(probT_psum, h - N_PROB + 1)
                    ve.tensor_tensor_reduce(prob_of(h)[:, 0:w], bank[2 * (n % 2) + z][:, 0:w],
                                            const("logmult")[:, SEQ - w:SEQ], -1.0, 3.0e38, ALU.add, ALU.min,
                                            neg_max[:, h:h + 1]).then_inc(masked_done, 1)

            def invert(n):
                dve.wait_ge(exp_done, 2 * n + 2)
                ve.reciprocal(row_inv[:, 2 * n:2 * n + 2], row_sum[:, 2 * n:2 * n + 2]).then_inc(inv_done, 1)

            def store_probT(n):
                dve.wait_ge(probT_psum, 2 * n + 1)
                if n >= 1:
                    dve.wait_ge(attn_psum, n)
                ve.tensor_copy(probT_of(n, 0)[:, 0:keys(n)], bank[4][:, 0:keys(n)]).then_inc(probT_done[0], 1)

            def store_attn_lo(n):
                i, m = divmod(n, PAIRS)
                dve.wait_ge(attn_hi_done, n + 1)
                if n >= OT_LO:
                    dve.wait_ge(mix_psum, 2 * ((n - OT_LO) // PAIRS + 1))
                ve.tensor_tensor(oT_lo[:, n % OT_LO, :], bank[6][:, 0:P],
                                 oT_hi[:, m, i * P:(i + 1) * P].bitcast(F32), ALU.subtract).then_inc(attn_done, 1)

            def add_mix(i, half):
                dve.wait_ge(mix_psum, 2 * i + half + 1)
                part = resid[:, i, half * 512:(half + 1) * 512]
                ve.tensor_tensor(part, part, bank[mix_bank(i, half)][:, :], ALU.add).then_inc(mix_done, 1)

            def keep_logits(i):
                dve.wait_ge(logit_psum, i + 1)
                ve.tensor_copy(logits[:, i, :], bank[7][:, 0:GROUPS + EXPERTS]).then_inc(logit_done, 1)

            steps = [0]

            def then(instruction):
                steps[0] += 1
                instruction.then_inc(rt_dve, 1)
                dve.wait_ge(rt_dve, steps[0])

            def wide(a, n):
                return a[:, :, None].to_broadcast([P, a.shape[1], n])

            def same(name, tiles, n):
                return const(name)[:, None, :].to_broadcast([P, tiles.stop - tiles.start, n])

            def candidates(tiles, part):
                n_log = GROUPS + EXPERTS
                logit, is_it, val = scaled[:, tiles], group_is[:, tiles], group_val[:, tiles]
                dve.wait_ge(std2_done, part + 1)
                ve.reciprocal(rstd2[:, tiles], std2[:, tiles]).then_inc(rstd2_ready, 1)
                dve.wait_ge(logit_done, tiles.stop)
                dve.wait_ge(rstd2_ready, part + 1)
                then(ve.tensor_tensor(logit, logits[:, tiles], wide(rstd2[:, tiles], n_log), ALU.mult))
                then(ve.tensor_tensor(logit, logit, same("bias", tiles, n_log), ALU.add))
                glog = logit[:, :, 0:GROUPS]
                then(ve.tensor_reduce(group_top[:, tiles], glog, AX.X, ALU.max))
                ve.tensor_tensor(group_low[:, tiles], glog, wide(group_top[:, tiles], GROUPS), ALU.subtract
                                 ).then_inc(low_ready, 1)
                then(ve.tensor_tensor(is_it, glog, wide(group_top[:, tiles], GROUPS), ALU.is_equal))
                then(ve.tensor_tensor(val, is_it, same("first8", tiles, GROUPS), ALU.mult))
                then(ve.tensor_reduce(group_first[:, tiles], val, AX.X, ALU.max))
                then(ve.tensor_tensor(is_it, val, wide(group_first[:, tiles], GROUPS), ALU.is_equal))
                then(ve.tensor_scalar(val, is_it, -NEVER, NEVER, ALU.mult, ALU.add))
                for t in range(tiles.start, tiles.stop):
                    last = ve.tensor_tensor(cand[:, t].rearrange("p (g e) -> p g e", g=GROUPS),
                                            scaled[:, t, GROUPS:n_log].rearrange("p (g e) -> p g e", g=GROUPS),
                                            group_val[:, t, :, None].to_broadcast([P, GROUPS, PER_GROUP]), ALU.add)
                    then(last)

            def choose(c, tiles):
                n, is_it, val = cand[:, tiles], is_top[:, tiles], top_val[:, tiles]
                then(ve.tensor_reduce(top[c][:, tiles], n, AX.X, ALU.max))
                then(ve.tensor_tensor(is_it, n, wide(top[c][:, tiles], EXPERTS), ALU.is_equal))
                then(ve.tensor_tensor(val, is_it, same("first64", tiles, EXPERTS), ALU.mult))
                then(ve.tensor_reduce(first[c][:, tiles], val, AX.X, ALU.max))
                then(ve.tensor_tensor(chosen[c][:, tiles], val, wide(first[c][:, tiles], EXPERTS), ALU.is_equal))
                if c == 0:
                    then(ve.scalar_tensor_tensor(n, chosen[0][:, tiles], 3 * NEVER, n, ALU.mult, ALU.add))
                else:
                    ve.tensor_tensor(picked[:, tiles], chosen[0][:, tiles], chosen[1][:, tiles], ALU.add
                                     ).then_inc(picked_ready, 1)

            def find_ranks(tiles, part):
                dve.wait_ge(rank_psum, part)
                then(ve.scalar_tensor_tensor(
                    ranked[:, tiles], bank[2][:, 0:TILES * EXPERTS].rearrange("p (t e) -> p t e", t=TILES)[:, tiles],
                    1.0, picked[:, tiles], ALU.add, ALU.mult))
                then(ve.tensor_scalar(rank[:, tiles, 0:EXPERTS], ranked[:, tiles], -1.0, None, ALU.add))

            def pick_set(b, column, tiles=slice(0, TILES)):
                shape = [P, tiles.stop - tiles.start, SET, SLOTS]
                return ve.tensor_tensor(pick[:, b, tiles].rearrange("p t (e s) -> p t e s", e=SET),
                                        slot_now[:, None, None, :].to_broadcast(shape),
                                        rank[:, tiles, bass.ds(column, SET)][:, :, :, None].to_broadcast(shape),
                                        ALU.is_equal)

            for n in range(UNITS + LAG):
                i, step = divmod(n - LAG - PAIRS, PAIRS)
                if i >= 0 and step in (2, 4):
                    add_mix(i, step // 2 - 1)
                if i >= 0 and step == 7:
                    keep_logits(i)
                if n < UNITS:
                    mask(n)
                if 1 <= n <= UNITS:
                    invert(n - 1)
                if n == UNITS + 2:
                    candidates(slice(0, TILES - 1), 0)
                if n >= LAG:
                    store_attn_lo(n - LAG)
                if 2 <= n < UNITS + 2:
                    store_probT(n - 2)
                if n < 2:
                    split_lo(HALVES - 2 + n)
                for g in range(W_OUT_PARTS):
                    if W_OUT_STEP[g] == n - 1:
                        split_lo(HALVES + g)
            choose(0, slice(0, TILES - 1))
            ve.tensor_copy(slot_now, const("slot")).then_inc(slot_ready, 1)
            add_mix(TILES - 1, 0)
            add_mix(TILES - 1, 1)
            choose(1, slice(0, TILES - 1))
            dve.sem_inc(added, 2)
            find_ranks(slice(0, TILES - 1), 1)
            dve.wait_ge(slot_ready, 1)
            pick_set(0, 0, slice(0, TILES - 1)).then_inc(pick_first, 1)
            keep_logits(TILES - 1)
            candidates(slice(TILES - 1, TILES), 1)
            for c in range(2):
                choose(c, slice(TILES - 1, TILES))
            ve.tensor_tensor(gap, top[1], top[0], ALU.subtract).then_inc(gap_ready, 1)

            find_ranks(slice(TILES - 1, TILES), 2)
            pick_set(0, 0, slice(TILES - 1, TILES)).then_inc(pick_done, 1)
            ve.tensor_scalar(rank[:, :, EXPERTS:EXPERTS + AHEAD], rank[:, :, 0:AHEAD], -float(SLOTS), None, ALU.add)
            then(ve.tensor_reduce(fullest, bank[3][:, 0:EXPERTS], AX.X, ALU.max))
            then(ve.tensor_scalar(is_round, const("round_start"), fullest, None, ALU.is_lt))
            then(ve.tensor_reduce(rounds_f, is_round, AX.X, ALU.add))
            ve.tensor_copy(counts_i[:, 1:2], rounds_f)
            ve.tensor_scalar(counts_i[:, 0:1], rounds_f, float(ITERS), None, ALU.mult).then_inc(routing_done, 1)
            pick_set(1, SET).then_inc(pick_done, 1)

            def store_first(half):
                dve.wait_ge(gather_psum, 2 * half + 2)
                chunks = slice(4 * half, 4 * half + 4)
                ve.tensor_tensor(xT[:, 0, chunks, :], bank[half][:, :].rearrange("p (c s) -> p c s", c=4),
                                 const("gain_ffn_gather")[:, chunks, None].to_broadcast([P, 4, P]),
                                 ALU.mult).then_inc(xT_done, 2)

            store_first(0)
            dve.wait_ge(gexp_done, 1)
            then(ve.tensor_reduce(group_sum, group_exp, AX.X, ALU.add))
            then(ve.reciprocal(group_prob, group_sum))
            store_first(1)
            dve.wait_ge(ratio_done, 1)
            then(ve.tensor_scalar(denom, ratio, 1.0, None, ALU.add))
            then(ve.reciprocal(inv, denom))
            then(ve.tensor_tensor(gate[0], inv, group_prob, ALU.mult))
            ve.tensor_tensor(gate[1], gate[0], ratio, ALU.mult).then_inc(gates_ready, 1)


            def store_xT(part, b):
                ps = bank[part % 2][:, 0:2 * P]
                ve.tensor_tensor(xT[:, b, 2 * part:2 * part + 2, :], ps.rearrange("p (c s) -> p c s", c=2),
                                 const("gain_ffn_gather")[:, 2 * part:2 * part + 2, None].to_broadcast([P, 2, P]),
                                 ALU.mult).then_inc(xT_done, 1)

            def add_back(t, half, b):
                part = resid[:, t, half * 512:(half + 1) * 512]
                return ve.tensor_tensor(part, part, bank[b][:, :], ALU.add)

            rounds = dve.value_load(counts_i[0:1, 1:2], min_val=1, max_val=MAX_ROUNDS)

            def vector_pass(r, it):
                for u in range(ITER):
                    b, e = divmod(u, SET)
                    done = r * EXPERTS + (it * ITER + u)
                    sets = r * (2 * ITERS) + (it * 2 + b)
                    for half in range(2):
                        dve.wait_ge(combine_psum, done * 2 + half + 1)
                        add_back(e, half, COMBINE_BANK[half]).then_inc(added, 1)
                    dve.wait_ge(silu_done, done + 1)
                    ve.tensor_tensor(hidden, hidden_gate, bank[2 + u % 2][:, P:2 * P], ALU.mult
                                     ).then_inc(hidden_done, 1)
                    dve.wait_ge(down_psum, done + 1)
                    for q in range(2, 4):
                        last = ve.tensor_copy(y_rows[SLOTS * e:SLOTS * (e + 1), b, q * 256:(q + 1) * 256],
                                              bank[6][SLOTS * q:SLOTS * (q + 1), 0:256])
                    last.then_inc(y_done_dve, 1)
                    dve.wait_ge(gather_psum, done + SET + 1)
                    store_xT(e, 1 - b)
                    if e == 1:
                        dve.wait_ge(gather_psum, sets * SET + SET)
                        dve.wait_ge(pickg_done, sets + 1)
                        pick_set(b, it * (2 * SET) + (AHEAD + b * SET)).then_inc(pick_done, 1)

            with dve.Fori(0, rounds) as r:
                with dve.Fori(0, ITERS) as it:
                    vector_pass(r, it)
                dve.wait_ge(pick_done, r * (2 * ITERS) + (2 * ITERS + 2))
                ve.tensor_scalar(slot_now, slot_now, float(SLOTS), None, ALU.add).then_inc(slot_ready, 1)
                dve.wait_ge(slot_ready, r + 2)
            for t in range(TILES):
                for half in range(2):
                    dve.wait_ge(combine_psum, rounds * (2 * EXPERTS) + (2 * t + half + 1))
                    add_back(t, half, final_bank(t, half)).then_inc(added, 1)

        @block.gpsimd
        def _(pool):
            gp = nc.gpsimd
            gp.memset(ones_bf[:, :], 1.0).then_inc(pool_step, 1)
            pool.wait_ge(pool_step, 1)
            gp.memset(kTz[DH:P, 0], 0.0).then_inc(pool_step, 1)
            pool.wait_ge(pool_step, 2)
            gp.memset(kTz[0:DH, 1], 0.0).then_inc(pool_step, 1)
            pool.wait_ge(pool_step, 3)
            pool.wait_ge(tables_in, 16)
            gp.tensor_copy(earlier_bf[:, :], const("earlier")).then_inc(pool_step, 1)
            pool.wait_ge(pool_step, 4)
            for n in range(UNITS):
                if n == EARLY_UNITS + 4:
                    pool.wait_ge(router_in, 16)
                    gp.tensor_tensor(router, router,
                                     const("gain_ffn_router")[:, :, None].to_broadcast([P, CHUNKS, P]), ALU.mult
                                     ).then_inc(tables_ready, 1)
                pool.wait_ge(inv_done, n + 1)
                for z in range(2):
                    h, w = 2 * n + z, keys(n)
                    gp.tensor_scalar(prob_of(h)[:, 0:w], prob_of(h)[:, 0:w], row_inv[:, h:h + 1], None,
                                     ALU.mult).then_inc(prob_done, 1)

            pool.wait_ge(low_ready, 2)
            gp.memset(y_rows[:, 1, :], 0.0).then_inc(y_done_dve, 1)
            pool.wait_ge(y_done_dve, 1)
            gp.memset(spread[:, 1], 0.0).then_inc(spread_done, 1)

            def gate_set(b, column):
                gp.tensor_tensor(pick_gated[:, b].rearrange("p t (e s) -> p t e s", e=SET),
                                 pick[:, b].rearrange("p t (e s) -> p t e s", e=SET),
                                 weight[:, :, bass.ds(column, SET)][:, :, :, None].to_broadcast(
                                     [P, TILES, SET, SLOTS]),
                                 ALU.mult).then_inc(pickg_done, 1)

            def wide(a):
                return a[:, :, None].to_broadcast([P, TILES, EXPERTS])

            pool.wait_ge(gates_ready, 1)
            gp.tensor_tensor(gated, chosen[0], wide(gate[0]), ALU.mult).then_inc(pool_step, 1)
            pool.wait_ge(pool_step, 5)
            gp.tensor_tensor(weight[:, :, 0:EXPERTS], chosen[1], wide(gate[1]), ALU.mult).then_inc(pool_step, 1)
            pool.wait_ge(pool_step, 6)
            gp.tensor_tensor(weight[:, :, 0:EXPERTS], weight[:, :, 0:EXPERTS], gated, ALU.add).then_inc(pool_step, 1)
            pool.wait_ge(pool_step, 7)
            gp.tensor_copy(weight[:, :, EXPERTS:EXPERTS + AHEAD], weight[:, :, 0:AHEAD]).then_inc(pool_step, 1)
            pool.wait_ge(pool_step, 8)
            pool.wait_ge(routing_done, 1)
            rounds = pool.value_load(counts_i[0:1, 1:2], min_val=1, max_val=MAX_ROUNDS)
            for b in range(2):
                pool.wait_ge(pick_done, b + 1)
                gate_set(b, b * SET)
            with pool.Fori(0, rounds) as r:
                with pool.Fori(0, ITERS) as it:
                    for b in range(2):
                        sets = r * (2 * ITERS) + it * 2 + b
                        pool.wait_ge(pick_done, sets + 3)
                        pool.wait_ge(spread_psum, sets + 1)
                        gate_set(b, it * (2 * SET) + (AHEAD + b * SET))


def kernel(**inputs):
    import concourse.bacc as bacc
    from concourse.bass_utils import run_bass_kernel_spmd

    a = {k: np.asarray(v) for k, v in inputs.items()}
    parts = constants()
    per_chunk = lambda g: g.reshape(CHUNKS, P).T
    parts["gain_mix"] = per_chunk(a["norm_mix"][0])
    parts["gain_ffn_router"] = per_chunk(a["norm_ffn"][0])
    parts["gain_ffn_gather"] = a["norm_ffn"][0].reshape(P, CHUNKS)
    parts["q_gain"] = np.tile(a["attn_q_norm"][0], 2)[:, None]
    parts["k_gain"] = np.tile(a["attn_k_norm"][0], 2)[:, None]
    parts["bias"] = np.tile(np.concatenate([a["moe_b_group"][0], a["moe_b_expert"][0]]), (P, 1))
    router = np.zeros((D, P), np.float32)
    router[:, 0:GROUPS] = a["moe_w_group"][0]
    router[:, GROUPS:GROUPS + EXPERTS] = a["moe_w_expert"][0]
    parts["router"] = router.reshape(CHUNKS, P, P).transpose(1, 0, 2).reshape(P, CHUNKS * P)
    params = np.empty((P, PARAMS), np.float32)
    for name, (lo, hi) in COLS.items():
        params[:, lo:hi] = parts[name]

    arrays = dict(x=a["x"][0], params=params, w_in=a["attn_w_in"][0], w_out=a["attn_w_out"][0],
                  w_gate=a["moe_w_gate"][0], w_up=a["moe_w_up"][0], w_down=a["moe_w_down"][0])
    arrays = {k: np.ascontiguousarray(v) for k, v in arrays.items()}
    nc = bacc.Bacc("TRN2", target_bir_lowering=False, num_devices=1)
    args = {k: nc.dram_tensor(k, v.shape, mybir.dt.from_np(v.dtype), kind="ExternalInput").ap()
            for k, v in arrays.items()}
    out = nc.dram_tensor("out", (SEQ, D), F32, kind="ExternalOutput").ap()
    trunk(nc, out=out, **args)
    result = run_bass_kernel_spmd(nc, [arrays], core_ids=[0])
    return result.results[0]["out"].reshape(1, SEQ, D)
```
